# Optimizing a Trainium2 kernel written in Bass

```python
import jax, jax.numpy as jnp
from jax import lax
import numpy as np

D_MODEL = 2048
BATCH = 1
SEQ = 256
DEPTH = 2

MIX_WIDTH = D_MODEL
HEAD_DIM = 128
ATTN_WIDTH = MIX_WIDTH // 2
N_HEADS = ATTN_WIDTH // HEAD_DIM
POOL_WIDTH = MIX_WIDTH - ATTN_WIDTH
POOL_WINDOWS = (2, 4, 8, 16)
N_POOL_GROUPS = len(POOL_WINDOWS)
POOL_GROUP = POOL_WIDTH // N_POOL_GROUPS
IN_WIDTH = 3 * ATTN_WIDTH + POOL_WIDTH
DILATED_CONFIGS = ((128, 1), (512, 4), (2048, 16))
Q_BLOCK = 64
ROPE_DIM = HEAD_DIM // 4
ROPE_THETA = 500000.0
D_FF = 4 * D_MODEL
EPS = 1e-6
NEG_BIG = -1e30

kernel_name = "hybrid_dilated_attn_multiscale_pool_encoder"

def rms_norm(x, g):
    xf = x.astype(jnp.float32)
    y = xf * lax.rsqrt(jnp.mean(xf * xf, axis=-1, keepdims=True) + EPS)
    return (y * g.astype(jnp.float32)).astype(x.dtype)

def partial_rope(x, positions):
    half = ROPE_DIM // 2
    inv_freq = jnp.power(ROPE_THETA, -jnp.arange(0, ROPE_DIM, 2, dtype=jnp.float32) / ROPE_DIM)
    ang = positions.astype(jnp.float32)[..., None] * inv_freq
    cos = jnp.cos(ang)[:, :, None, :]
    sin = jnp.sin(ang)[:, :, None, :]
    xr = x[..., :ROPE_DIM].astype(jnp.float32)
    x1, x2 = xr[..., :half], xr[..., half:]
    rot = jnp.concatenate([x1 * cos - x2 * sin, x2 * cos + x1 * sin], axis=-1)
    return jnp.concatenate([rot.astype(x.dtype), x[..., ROPE_DIM:]], axis=-1)

def dilated_window_attention(q, k, v, window, dilation):
    B, S, H, Dh = q.shape
    half = window // (2 * dilation)
    L = S // dilation
    nb = -(-L // Q_BLOCK)
    Lp = nb * Q_BLOCK
    kw = Q_BLOCK + 2 * half

    def to_sub(t):
        t = t.reshape(B, L, dilation, H, Dh).transpose(0, 2, 3, 1, 4)
        return jnp.pad(t, ((0, 0), (0, 0), (0, 0), (0, Lp - L), (0, 0)))

    qs, ks, vs = to_sub(q), to_sub(k), to_sub(v)
    qb = qs.reshape(B, dilation, H, nb, Q_BLOCK, Dh) * (Dh ** -0.5)
    pad = ((0, 0), (0, 0), (0, 0), (half, half), (0, 0))
    idx = jnp.arange(nb)[:, None] * Q_BLOCK + jnp.arange(kw)[None, :]
    kb = jnp.take(jnp.pad(ks, pad), idx, axis=3)
    vb = jnp.take(jnp.pad(vs, pad), idx, axis=3)

    s = jnp.einsum('brhnqd,brhnkd->brhnqk', qb, kb).astype(jnp.float32)
    key_pos = idx - half
    q_pos = jnp.arange(nb)[:, None] * Q_BLOCK + jnp.arange(Q_BLOCK)[None, :]
    rel = key_pos[:, None, :] - q_pos[:, :, None]
    valid = (jnp.abs(rel) <= half) & (key_pos[:, None, :] >= 0) & (key_pos[:, None, :] < L)
    s = jnp.where(valid, s, NEG_BIG)
    m = jnp.max(s, axis=-1, keepdims=True)
    p = jnp.exp(s - m)
    den = jnp.sum(p, axis=-1, keepdims=True)
    o = jnp.einsum('brhnqk,brhnkd->brhnqd', p.astype(vb.dtype), vb).astype(jnp.float32) / den
    lse = (m + jnp.log(den))[..., 0]

    o = o.reshape(B, dilation, H, Lp, Dh)[:, :, :, :L].transpose(0, 3, 1, 2, 4).reshape(B, S, H, Dh)
    lse = lse.reshape(B, dilation, H, Lp)[:, :, :, :L].transpose(0, 3, 1, 2).reshape(B, S, H)
    return o, lse

def dilated_mixture_attention(q, k, v):
    outs, lses = [], []
    for window, dilation in DILATED_CONFIGS:
        o, lse = dilated_window_attention(q, k, v, window, dilation)
        outs.append(o)
        lses.append(lse)
    w = jax.nn.softmax(jnp.stack(lses, axis=0), axis=0)
    out = jnp.sum(w[..., None] * jnp.stack(outs, axis=0), axis=0)
    return out.astype(q.dtype)

def multiscale_pool(u, w_pool, pool_scale):
    B, S, _ = u.shape
    uf = u.reshape(B, S, N_POOL_GROUPS, POOL_GROUP).astype(jnp.float32)
    c = jnp.pad(jnp.cumsum(uf, axis=1), ((0, 0), (1, 0), (0, 0), (0, 0)))
    pos = jnp.arange(S)
    outs = []
    for g, win in enumerate(POOL_WINDOWS):
        lo = jnp.clip(pos - win // 2, 0, S)
        hi = jnp.clip(pos + win // 2, 0, S)
        cnt = (hi - lo).astype(jnp.float32)[None, :, None]
        mean = (c[:, hi, g] - c[:, lo, g]) / cnt
        outs.append(mean - uf[:, :, g])
    pooled = jnp.stack(outs, axis=2).astype(u.dtype)
    y = jnp.einsum('bsgc,gcd->bsgd', pooled, w_pool)
    return y.reshape(B, S, POOL_WIDTH) * pool_scale

def hybrid_layer(x, positions, g_mix_pre, w_in, g_attn_out, w_pool, pool_scale, g_pool_out,
                 w_out, g_mix_post, g_ffn_pre, w_up, w_down, g_ffn_post):
    B, S, _ = x.shape
    h = rms_norm(x, g_mix_pre)
    proj = h @ w_in
    q = proj[..., :ATTN_WIDTH].reshape(B, S, N_HEADS, HEAD_DIM)
    k = proj[..., ATTN_WIDTH:2 * ATTN_WIDTH].reshape(B, S, N_HEADS, HEAD_DIM)
    v = proj[..., 2 * ATTN_WIDTH:3 * ATTN_WIDTH].reshape(B, S, N_HEADS, HEAD_DIM)
    u = proj[..., 3 * ATTN_WIDTH:]
    q = partial_rope(q, positions)
    k = partial_rope(k, positions)
    attn = dilated_mixture_attention(q, k, v).reshape(B, S, ATTN_WIDTH)
    pool = multiscale_pool(u, w_pool, pool_scale)
    mixed = jnp.concatenate([rms_norm(attn, g_attn_out), rms_norm(pool, g_pool_out)], axis=-1) @ w_out
    x = x + rms_norm(mixed, g_mix_post)
    f = jnp.square(jax.nn.relu(rms_norm(x, g_ffn_pre) @ w_up)) @ w_down
    return x + rms_norm(f, g_ffn_post)

def setup_inputs(seed: int = 0) -> dict:
    key = jax.random.key(seed)
    ks = jax.random.split(key, 16)
    f32 = jnp.float32

    def gain(k, n):
        return 1.0 + 0.05 * jax.random.normal(k, (DEPTH, n), f32)

    x = jax.random.normal(ks[0], (BATCH, SEQ, D_MODEL), f32)
    positions = jnp.broadcast_to(jnp.arange(SEQ, dtype=jnp.int32), (BATCH, SEQ))
    return {
        "x": x,
        "positions": positions,
        "g_mix_pre": gain(ks[1], D_MODEL),
        "w_in": jax.random.normal(ks[2], (DEPTH, D_MODEL, IN_WIDTH), f32) * D_MODEL ** -0.5,
        "g_attn_out": gain(ks[3], ATTN_WIDTH),
        "w_pool": jax.random.normal(ks[4], (DEPTH, N_POOL_GROUPS, POOL_GROUP, POOL_GROUP), f32) * POOL_GROUP ** -0.5,
        "pool_scale": 1.0 + 0.1 * jax.random.normal(ks[5], (DEPTH, POOL_WIDTH), f32),
        "g_pool_out": gain(ks[6], POOL_WIDTH),
        "w_out": jax.random.normal(ks[7], (DEPTH, MIX_WIDTH, D_MODEL), f32) * MIX_WIDTH ** -0.5,
        "g_mix_post": gain(ks[8], D_MODEL),
        "g_ffn_pre": gain(ks[9], D_MODEL),
        "w_up": jax.random.normal(ks[10], (DEPTH, D_MODEL, D_FF), f32) * D_MODEL ** -0.5,
        "w_down": jax.random.normal(ks[11], (DEPTH, D_FF, D_MODEL), f32) * D_FF ** -0.5,
        "g_ffn_post": gain(ks[12], D_MODEL),
    }

def reference(x, positions, g_mix_pre, w_in, g_attn_out, w_pool, pool_scale, g_pool_out,
              w_out, g_mix_post, g_ffn_pre, w_up, w_down, g_ffn_post):
    for l in range(DEPTH):
        x = hybrid_layer(x, positions, g_mix_pre[l], w_in[l], g_attn_out[l], w_pool[l],
                         pool_scale[l], g_pool_out[l], w_out[l], g_mix_post[l], g_ffn_pre[l],
                         w_up[l], w_down[l], g_ffn_post[l])
    return x


_drawn_inputs = setup_inputs


def setup_inputs(seed=0):
    import zlib

    import numpy as np

    out = dict(_drawn_inputs(seed))
    spreads = {}
    factors = {}
    for name, (base, spread) in spreads.items():
        noise = np.random.default_rng([zlib.crc32(name.encode()), seed]).standard_normal(out[name].shape)
        drawn = base * np.exp(spread * noise) if base else spread * noise
        out[name] = __import__('jax').numpy.asarray(drawn.astype(out[name].dtype))
    for name, factor in factors.items():
        out[name] = (out[name] * factor).astype(out[name].dtype)
    return out
```

```python
import numpy as np

import concourse.bass as bass
from concourse import mybir

F32 = mybir.dt.float32
F32R = mybir.dt.float32r
I32 = mybir.dt.int32
ALU = mybir.AluOpType
ACT = mybir.ActivationFunctionType
AX = mybir.AxisListType

P = 128
D = 2048
SEQ = 256
DEPTH = 2
T = SEQ // P
HALF_W = D // 2
HEADS = HALF_W // 128
WINDOWS = (2, 4, 8, 16)
GROUP = HALF_W // len(WINDOWS)
D_FF = 4 * D
ROPE = 32
THETA = 500000.0
EPS = 1e-6
NEG_BIG = -1e30
CH = 512
KT = D // P
PAIRS = 4
FF_GROUPS = D_FF // D
UNITS_A = 8
CHUNKS = D // CH

HU_B1 = 2 * UNITS_A
HU_B2 = HU_B1 + CHUNKS
HU_F = HU_B2 + CHUNKS
HU_GROUP = 4 * CHUNKS
HU_LAYER = HU_F + FF_GROUPS * HU_GROUP
PAIRS_LAYER = PAIRS * HU_LAYER

ACC_B1 = UNITS_A
ACC_B2 = ACC_B1 + CHUNKS
ACC_F = ACC_B2 + CHUNKS
ACC_LAYER = ACC_F + FF_GROUPS * 2 * CHUNKS

TB_Y = 4
TB_QK = 6
TB_H2 = 14
TB_F = 18
TB_LAYER = TB_F + FF_GROUPS * CHUNKS

XG_Y = 8
XG_O = 12
XG_H2 = 16
XG_LAYER = 24

SQ_Y = 8
SQ_B2 = 10
SQ_H2 = 18
SQ_F = 26
SQ_LAYER = 34
RS_X1, RS_P, RS_A, RS_POST1, RS_X2, RS_POST2 = 0, 2, 3, 4, 6, 8
RS_LAYER = 10
COL_X1, COL_P, COL_A, COL_POST1, COL_X2, COL_POST2 = 0, 2, 4, 6, 8, 10

G_MIX, G_ATTN, G_POOL, G_FFN, G_LAYER = 0, 16, 24, 32, 48

H_ORDER = [(0, 0), (0, 1), (1, 0), (1, 1), (0, 2), (0, 3), (1, 2), (1, 3)]
Y_ORDER = [(0, 0), (1, 0), (0, 1), (1, 1)]

BAND = P + max(WINDOWS) // 2
BAND_AT = SEQ - BAND

RING = 2 * PAIRS
RAW = PAIRS
XG_SLOTS = 2
T_INIT = 2 * CHUNKS


def trunc_bits(v, bits):
    m, e = np.frexp(v)
    return float(np.ldexp(np.trunc(np.ldexp(m, bits)), int(e) - bits))


def build(nc, x_in, positions, g_mix_pre, w_in, g_attn_out, w_pool, pool_scale, g_pool_out,
          w_out, g_mix_post, g_ffn_pre, w_up, w_down, g_ffn_post, out):
    top = [((nc.sbuf_base + 31) // 32) * 32]

    def region(nbytes):
        at = top[0]
        top[0] += (nbytes + 31) // 32 * 32
        assert top[0] <= nc.sbuf_usable_end, top[0]
        return at

    def at(name, shape, dtype, offset):
        return nc.alloc_sbuf_tensor_at(name, shape, dtype, offset=offset)

    def own(name, shape, dtype=F32):
        return at(name, shape, dtype, region(4 * int(np.prod(shape[1:]))))

    x = own("x", [P, T, D])
    raw = own("raw", [P, RAW, 2 * CH])
    w_hi = own("w_hi", [P, RING, 2 * CH], F32R)
    w_lo = own("w_lo", [P, RING, 2 * CH], F32R)
    r_h = region(2 * 4 * KT * SEQ)
    h_hi = at("h_hi", [P, KT, SEQ], F32R, r_h)
    h_lo = at("h_lo", [P, KT, SEQ], F32R, r_h + 4 * KT * SEQ)
    qk_t = at("qk_t", [P, 2, 2 * SEQ], F32, r_h)
    probs = at("probs", [P, 2, T, SEQ], F32, r_h + 4096)
    probs_t = at("probs_t", [P, 2, T, SEQ], F32, r_h + 8192)
    o_sq = at("o_sq", [P, 2 * SEQ], F32, r_h + 12288)
    o_sqsum = at("o_sqsum", [P, 2 * SEQ], F32, r_h + 14336)
    r_f = region(2 * 4 * KT * SEQ)
    f_hi = at("f_hi", [P, KT, SEQ], F32R, r_f)
    f_lo = at("f_lo", [P, KT, SEQ], F32R, r_f + 4 * KT * SEQ)
    w_pool_s = at("w_pool_s", [P, len(WINDOWS) * 2, GROUP], F32, r_f)
    scale_row = at("scale_row", [P, HALF_W], F32, r_f + 4 * KT * SEQ)
    r_acc = region(4 * T * D)
    acc = at("acc", [P, T, D], F32, r_acc)
    pooled_t = at("pooled_t", [P, 2 * len(WINDOWS), SEQ], F32, r_acc)
    tmp_i = at("tmp_i", [P, T, SEQ], I32, r_acc)
    tmp = [at(f"tmp{n}", [P, T, SEQ], F32, r_acc + 2048 * (n + 1)) for n in range(3)]
    r_qkv = region(4 * 6 * T * CH)
    assert r_qkv == r_acc + 4 * T * D
    proj = at("proj", [P, UNITS_A, T, CH], F32, r_acc + 4 * D)
    y = at("y", [P, 2, T, CH], F32, r_acc + 4 * D)
    junk = at("junk", [P, CH], F32, r_qkv + 4 * T * CH)
    junk_y = at("junk_y", [P, 2, CH], F32, r_acc)
    act_f = at("act_f", [P, T, CH], F32, r_qkv)
    post_row = own("post_row", [P, D])
    r_xg = region(4 * XG_SLOTS * CH)
    xg = at("xg", [P, XG_SLOTS, CH], F32, r_xg)
    rope_tmp = at("rope_tmp", [P, 4, 4, 4, ROPE // 2], F32, r_xg)
    ident = own("ident", [P, P])
    bias = own("bias", [P, T, SEQ])
    band = own("band", [P, len(WINDOWS), T, BAND])
    gain_rows = at("gain_rows", [DEPTH * G_LAYER, P], F32, r_h)
    gains = own("gains", [P, DEPTH * G_LAYER])
    gain = own("gain", [P, G_LAYER])
    cos_t = own("cos_t", [P, T, ROPE // 2])
    sin_t = own("sin_t", [P, T, ROPE // 2])
    pos_i = own("pos_i", [P, T], I32)
    ss_x = own("ss_x", [P, T, CHUNKS])
    ss_post = own("ss_post", [P, T, CHUNKS])
    ss_p = own("ss_p", [P, T])
    mean_sq = own("mean_sq", [P, 12])
    rstd = own("rstd", [P, 12])
    neg_max = own("neg_max", [P, HEADS, T])
    den = own("den", [P, HEADS, T])
    rden = own("rden", [P, HEADS, T])
    minus_half = own("minus_half", [P, 2])
    ones = own("ones", [P, 1])
    rt = [own(f"rt{n}", [P, T, ROPE // 2]) for n in range(6)]
    rt_i = own("rt_i", [P, T, ROPE // 2], I32)
    pos_f = own("pos_f", [P, T])
    freq = own("freq", [P, ROPE // 2])

    acc_bank = [nc.alloc_psum_tensor(f"acc_bank{t}", [P, CH], F32) for t in range(T)]
    t_bank = [nc.alloc_psum_tensor(f"t_bank{n}", [P, CH], F32) for n in range(2)]
    s_bank = [nc.alloc_psum_tensor(f"s_bank{n}", [P, CH], F32) for n in range(2)]
    o_bank = nc.alloc_psum_tensor("o_bank", [P, CH], F32)
    ssa_bank = nc.alloc_psum_tensor("ssa_bank", [P, CH], F32)

    sem = nc.alloc_semaphore
    gains_loaded, x_loaded, pos_loaded = sem("gains_loaded"), sem("x_loaded"), sem("pos_loaded")
    raw_loaded = [sem(f"raw_loaded{p}") for p in range(RAW)]
    pool_w_loaded, scale_loaded = sem("pool_w_loaded"), sem("scale_loaded")
    post_row_loaded = sem("post_row_loaded")
    stored = sem("stored")
    hi_made, lo_made, w_used = sem("hi_made"), sem("lo_made"), sem("w_used")
    acc_done = sem("acc_done")
    acc_free = [sem(f"acc_free{t}") for t in range(T)]
    tb_done = [sem(f"tb_done{n}") for n in range(2)]
    tb_free = [sem(f"tb_free{n}") for n in range(2)]
    x_ready, xg_ready = sem("x_ready"), sem("xg_ready")
    st_hi, st_lo = sem("st_hi"), sem("st_lo")
    sq_done, mean_ready, rstd_ready = sem("sq_done"), sem("mean_ready"), sem("rstd_ready")
    post_ready = sem("post_ready")
    relu_done, f_ready, fhi_made, flo_made = (sem("relu_done"), sem("f_ready"), sem("fhi_made"),
                                              sem("flo_made"))
    setup_done, gains_turned, gains_ready, gain_ready = (sem("setup_done"), sem("gains_turned"),
                                                         sem("gains_ready"), sem("gain_ready"))
    ident_made, table_step, band_ready, bias_ready = (sem("ident_made"), sem("table_step"),
                                                      sem("band_ready"), sem("bias_ready"))
    angle_ready, rope_table_ready = sem("angle_ready"), sem("rope_table_ready")
    pooled_done, pooled_ready, y_done, y_ready = (sem("pooled_done"), sem("pooled_ready"),
                                                  sem("y_done"), sem("y_ready"))
    rope_step = sem("rope_step")
    s_done, score_ready, max_ready = sem("s_done"), sem("score_ready"), sem("max_ready")
    exp_done, rden_ready, prob_ready = sem("exp_done"), sem("rden_ready"), sem("prob_ready")
    o_done, o_squared, o_summed = sem("o_done"), sem("o_squared"), sem("o_summed")
    ssa_done = sem("ssa_done")

    def h_cols(t):
        return slice(t * P, (t + 1) * P)

    def c_cols(c):
        return slice(c * CH, (c + 1) * CH)

    ld = bass.ds

    def f_out(dst, u, t):
        return dst[:, ld(u * 4, 4), h_cols(t)]

    def result_stands(eng, t, result, hu):
        if t == 0:
            eng.wait_ge(acc_done, result + 1)
        else:
            eng.wait_ge(w_used, RING + PAIRS * hu + PAIRS)

    with nc.Block() as block:

        @block.sync
        def _(sp):
            for l in range(DEPTH):
                for at_row, g, n in ((G_MIX, g_mix_pre, 16), (G_ATTN, g_attn_out, 8),
                                     (G_POOL, g_pool_out, 8), (G_FFN, g_ffn_pre, 16)):
                    r = l * G_LAYER + at_row
                    sp.dma_start(gain_rows[r:r + n, :],
                                 g[l].rearrange("(k p) -> k p", p=P)).then_inc(gains_loaded, 16)
            x_rows = x_in[0].rearrange("(t p) d -> t p d", p=P)
            for t in range(T):
                sp.dma_start(x[:, t, :], x_rows[t]).then_inc(x_loaded, 16)
            sp.dma_start(pos_i[:, :], positions[0].rearrange("(t p) -> p t", p=P),
                         allow_slow_non_contiguous=True).then_inc(pos_loaded, 16)

            def load_half(w, l, row, col, hu):
                for p in range(PAIRS):
                    sp.wait_ge(lo_made, hu * PAIRS + p + 1)
                    src = w[ld(l, 1), ld(row + p * 2 * P, 2 * P), ld(col, CH)]
                    sp.dma_start(raw[:, p, :].rearrange("p (k c) -> p k c", k=2),
                                 src.rearrange("a (k p) c -> p (a k) c", p=P)
                                 ).then_inc(raw_loaded[p], 16)

            def load_unit(w, l, row, col, hu):
                load_half(w, l, row, col, hu)
                load_half(w, l, row + HALF_W, col, hu + 1)

            def load_post_row(g, l):
                src = g[ld(l, 1), :].to_broadcast([P, D])
                sp.dma_start(post_row[:, :], src).then_inc(post_row_loaded, 16)

            def load_group(l, g):
                hu = l * HU_LAYER + HU_F + g * HU_GROUP
                with sp.Fori(0, CHUNKS) as u:
                    load_unit(w_up, l, 0, g * D + u * CH, hu + u * 2)
                with sp.Fori(0, CHUNKS) as c:
                    load_unit(w_down, l, g * D, c * CH, hu + 2 * CHUNKS + c * 2)

            with sp.Fori(0, DEPTH) as l:
                hu = l * HU_LAYER
                with sp.Fori(0, 2) as u:
                    load_unit(w_in, l, 0, 3 * HALF_W + u * CH, hu + u * 2)
                sp.wait_ge(acc_done, l * ACC_LAYER + 1)
                sp.dma_start(w_pool_s[:, :, :],
                             w_pool[ld(l, 1)].rearrange("a g (c p) d -> p (a g c) d", p=P)
                             ).then_inc(pool_w_loaded, 16)
                sp.dma_start(scale_row[:, :], pool_scale[ld(l, 1), :].to_broadcast([P, HALF_W])
                             ).then_inc(scale_loaded, 16)
                with sp.Fori(0, 6) as u:
                    load_unit(w_in, l, 0, u * CH, hu + 4 + u * 2)
                sp.wait_ge(post_ready, T_INIT + l * 4 * CHUNKS)
                load_post_row(g_mix_post, l)
                with sp.Fori(0, CHUNKS) as c:
                    load_half(w_out, l, HALF_W, c * CH, hu + HU_B1 + c)
                with sp.Fori(0, CHUNKS) as c:
                    load_half(w_out, l, 0, c * CH, hu + HU_B2 + c)
                with sp.Fori(0, FF_GROUPS - 1) as g:
                    load_group(l, g)
                sp.wait_ge(post_ready, T_INIT + l * 4 * CHUNKS + 2 * CHUNKS)
                load_post_row(g_ffn_post, l)
                load_group(l, FF_GROUPS - 1)

            out_rows = out[0].rearrange("(t p) d -> t p d", p=P)
            for t in range(T):
                for c in range(CHUNKS):
                    sp.wait_ge(x_ready, 16 * DEPTH + H_ORDER.index((t, c)) + 1)
                    sp.dma_start(out_rows[t][:, c_cols(c)], x[:, t, c_cols(c)]).then_inc(stored, 16)
            sp.wait_ge(stored, 16 * T * CHUNKS)

        @block.tensor
        def _(pe):
            def pairs(t, hu, half, hi, lo, k0, first, last, result, which=range(PAIRS), need=None):
                for p in which:
                    slot = half * PAIRS + p
                    if need is not None:
                        need(p)
                    if first and p == 0:
                        pe.wait_ge(acc_free[t], result + 1)
                    if t == 0:
                        pe.wait_ge(lo_made, hu * PAIRS + p + 1 + RAW)
                    for k in range(2):
                        kt = k0 + 2 * p + k
                        xh, xl = hi[:, kt, h_cols(t)], lo[:, kt, h_cols(t)]
                        wh = w_hi[:, slot, c_cols(k)]
                        wl = w_lo[:, slot, c_cols(k)]
                        begin = first and p == 0 and k == 0
                        end = last and p == PAIRS - 1 and k == 1
                        pe.matmul(acc_bank[t][:, :], xh, wh, start=begin, stop=False)
                        pe.matmul(acc_bank[t][:, :], xh, wl, start=False, stop=False)
                        mm = pe.matmul(acc_bank[t][:, :], xl, wh, start=False, stop=end)
                    if t == 1:
                        mm.then_inc(w_used, 1)
                    elif last and p == PAIRS - 1:
                        mm.then_inc(acc_done, 1)

            def unit(hu, result, hi, lo, gap):
                for half in range(2):
                    for t in range(T):
                        gap(2 * half + t)
                        pairs(t, hu + half, half, hi, lo, 8 * half, half == 0, half == 1, result)

            def h_turns(l, h):
                def gap(n):
                    for i in (2 * n, 2 * n + 1):
                        t, c = H_ORDER[i]
                        pe.wait_ge(x_ready, l * 16 + 8 * h + i + 1)
                        if i >= 2:
                            pe.wait_ge(xg_ready, l * XG_LAYER + (0, XG_H2)[h] + i - 1)
                        for j in range(4):
                            tr = pe.transpose(t_bank[i % 2][:, h_cols(j)],
                                              x[:, t, c * CH + j * P:c * CH + (j + 1) * P],
                                              ident[:, :])
                        tr.then_inc(tb_done[i % 2], 1)
                    pe.wait_ge(st_lo, XG_SLOTS + l * XG_LAYER + (0, XG_H2)[h] + 2 * n + 2)
                return gap

            def no_gap(n):
                pass

            pe.sem_inc(w_used, RING)
            for n in range(2):
                pe.sem_inc(acc_free[n], 1)
            pe.wait_ge(ident_made, 2)
            pe.wait_ge(gains_loaded, 16 * 4 * DEPTH)
            pe.transpose(s_bank[0][:, 0:DEPTH * G_LAYER], gain_rows[:, :],
                         ident[0:DEPTH * G_LAYER, 0:DEPTH * G_LAYER]).then_inc(gains_turned, 1)

            with pe.Fori(0, DEPTH) as l:
                hu0 = l * HU_LAYER
                a0 = l * ACC_LAYER
                xg0 = XG_SLOTS + l * XG_LAYER

                unit(hu0, a0, h_hi, h_lo, h_turns(l, 0))
                with pe.Fori(1, 6) as u:
                    unit(hu0 + u * 2, a0 + u, h_hi, h_lo, no_gap)

                def pooled(g):
                    if g >= 2:
                        pe.wait_ge(pooled_ready, l * 4 + g - 1)
                    for ct in range(2):
                        ch = g * GROUP + ct * P
                        src = [proj[:, ch // CH, t, ch % CH:ch % CH + P] for t in range(T)]
                        dst = s_bank[g % 2]
                        o = ct * SEQ
                        pe.matmul(dst[:, o:o + BAND_AT], src[0], band[:, g, 0, 0:BAND_AT],
                                  start=True, stop=True)
                        pe.matmul(dst[:, o + BAND:o + SEQ], src[1], band[:, g, 1, BAND - BAND_AT:BAND],
                                  start=True, stop=True)
                        pe.matmul(dst[:, o + BAND_AT:o + BAND], src[0], band[:, g, 0, BAND_AT:BAND],
                                  start=True, stop=False)
                        mm = pe.matmul(dst[:, o + BAND_AT:o + BAND], src[1],
                                       band[:, g, 1, 0:BAND - BAND_AT], start=False, stop=True)
                    mm.then_inc(pooled_done, 1)

                def pool_out(g):
                    pe.wait_ge(pooled_ready, l * 4 + g + 1)
                    if g < 2:
                        pe.wait_ge(pooled_ready, l * 4 + g + 3)
                    else:
                        pe.wait_ge(y_ready, l * 4 + g - 1)
                    for t in range(T):
                        for ct in range(2):
                            mm = pe.matmul(s_bank[g % 2][:, t * GROUP:(t + 1) * GROUP],
                                           pooled_t[:, 2 * g + ct, h_cols(t)],
                                           w_pool_s[:, 2 * g + ct, :], start=ct == 0, stop=ct == 1)
                    mm.then_inc(y_done, 1)

                def y_turn(i):
                    t, c = Y_ORDER[i]
                    pe.wait_ge(y_ready, l * 4 + 2 * c + 2)
                    if i >= 2:
                        pe.wait_ge(xg_ready, l * XG_LAYER + XG_Y + i - 1)
                    for j in range(4):
                        tr = pe.transpose(t_bank[i % 2][:, h_cols(j)],
                                          y[:, c, t, h_cols(j)], ident[:, :])
                    tr.then_inc(tb_done[i % 2], 1)

                def gap_v0(n):
                    if n == 1:
                        for t in range(T):
                            pe.wait_ge(acc_free[t], a0 + 2 + 1)
                        pe.wait_ge(band_ready, 1)
                    if n in (1, 2):
                        pooled(2 * n - 2)
                        pooled(2 * n - 1)
                    if n == 3:
                        pe.wait_ge(pool_w_loaded, l * 16 + 16)
                        pool_out(0)
                        pool_out(1)

                def gap_v1(n):
                    if n == 0:
                        pool_out(2)
                        pool_out(3)
                    if n in (1, 2):
                        y_turn(2 * n - 2)
                        y_turn(2 * n - 1)

                unit(hu0 + 12, a0 + 6, h_hi, h_lo, gap_v0)
                unit(hu0 + 14, a0 + 7, h_hi, h_lo, gap_v1)

                def turn_qk(c):
                    if c == 0:
                        pe.wait_ge(rope_step, l * 12 + 12)
                    for e in range(2):
                        h = 2 * c + e
                        if c > 0:
                            pe.wait_ge(tb_free[e], l * 8 + 2 * c)
                        for n, first_unit in enumerate((2, 4)):
                            for t in range(T):
                                tr = pe.transpose(
                                    t_bank[e][:, n * SEQ + t * P:n * SEQ + (t + 1) * P],
                                    proj[:, first_unit + h // 4, t, h_cols(h % 4)], ident[:, :])
                        tr.then_inc(tb_done[e], 1)

                def scores(c):
                    for e in range(2):
                        pe.wait_ge(tb_free[e], l * 8 + 2 * c + 1)
                        if c == 0:
                            pe.wait_ge(y_ready, l * 4 + 3 + e)
                        else:
                            pe.wait_ge(score_ready, l * HEADS + 2 * c + e - 1)
                        for t in range(T):
                            mm = pe.matmul(s_bank[e][:, t * SEQ:(t + 1) * SEQ],
                                           qk_t[:, e, h_cols(t)], qk_t[:, e, SEQ:2 * SEQ],
                                           start=True, stop=True)
                        mm.then_inc(s_done, 1)

                def turn_probs(c):
                    for e in range(2):
                        pe.wait_ge(prob_ready, l * HEADS + 2 * c + e + 1)
                        pe.wait_ge(tb_free[e], l * 8 + 2 * c + 1)
                        for kt in range(T):
                            for t in range(T):
                                tr = pe.transpose(
                                    t_bank[e][:, kt * SEQ + t * P:kt * SEQ + (t + 1) * P],
                                    probs[:, e, t, h_cols(kt)], ident[:, :])
                        tr.then_inc(tb_done[e], 1)

                def mix_values(c):
                    if c == 0:
                        for t in range(T):
                            pe.wait_ge(acc_free[t], a0 + 8 + 1)
                    else:
                        pe.wait_ge(xg_ready, l * XG_LAYER + XG_O + c)
                        pe.wait_ge(o_squared, l * 4 + c)
                    for e in range(2):
                        h = 2 * c + e
                        pe.wait_ge(tb_free[e], l * 8 + 2 * c + 2)
                        for kt in range(T):
                            mm = pe.matmul(o_bank[:, e * SEQ:(e + 1) * SEQ],
                                           proj[:, 6 + h // 4, kt, h_cols(h % 4)],
                                           probs_t[:, e, kt, :], start=kt == 0, stop=kt == 1)
                    mm.then_inc(o_done, 1)

                for c in range(CHUNKS):
                    hu, half = hu0 + HU_B1 + c, c % 2
                    if c == 0:
                        pe.wait_ge(st_lo, xg0 + XG_O)
                    pairs(0, hu, half, f_hi, f_lo, 8, True, True, a0 + ACC_B1 + c, (0, 1))
                    if c > 0:
                        mix_values(c - 1)
                    turn_qk(c)
                    pairs(0, hu, half, f_hi, f_lo, 8, True, True, a0 + ACC_B1 + c, (2, 3))
                    scores(c)
                    pairs(1, hu, half, f_hi, f_lo, 8, True, True, a0 + ACC_B1 + c)
                    turn_probs(c)

                for c in range(CHUNKS):
                    hu, half = hu0 + HU_B2 + c, c % 2
                    if c == 0:
                        def heads_ready(p):
                            pe.wait_ge(st_lo, xg0 + XG_O + p + 1)
                        pairs(0, hu, half, f_hi, f_lo, 0, True, True, a0 + ACC_B2 + c, (0, 1),
                              heads_ready)
                        mix_values(CHUNKS - 1)
                        pairs(0, hu, half, f_hi, f_lo, 0, True, True, a0 + ACC_B2 + c, (2, 3),
                              heads_ready)
                        pe.wait_ge(o_summed, l * 4 + 4)
                        for t in range(T):
                            for e in range(2):
                                mm = pe.matmul(ssa_bank[:, t:t + 1],
                                               o_sqsum[:, e * SEQ + t * P:e * SEQ + (t + 1) * P],
                                               ones[:, :], start=e == 0, stop=e == 1)
                        mm.then_inc(ssa_done, 1)
                    else:
                        pairs(0, hu, half, f_hi, f_lo, 0, True, True, a0 + ACC_B2 + c)
                    pairs(1, hu, half, f_hi, f_lo, 0, True, True, a0 + ACC_B2 + c)

                def turn_f(g, u, t):
                    pe.wait_ge(f_ready, l * 32 + g * 8 + u * 2 + t + 1)
                    pe.wait_ge(flo_made, l * 32 + g * 8 + u * 2 + t + 1)
                    for j in range(4):
                        tr = pe.transpose(t_bank[t][:, h_cols(j)], act_f[:, t, h_cols(j)],
                                          ident[:, :])
                    tr.then_inc(tb_done[t], 1)

                def group(g, first_gap):
                    hu = hu0 + HU_F + g * HU_GROUP
                    r = a0 + ACC_F + g * (2 * CHUNKS)
                    unit(hu, r, h_hi, h_lo, first_gap)
                    turn_f(g, 0, 0)
                    with pe.Fori(1, CHUNKS) as u:
                        def gap_up(n):
                            if n == 1:
                                turn_f(g, u - 1, 1)
                        unit(hu + u * 2, r + u, h_hi, h_lo, gap_up)
                        turn_f(g, u, 0)

                    def gap_down(n):
                        if n == 1:
                            turn_f(g, CHUNKS - 1, 1)
                        pe.wait_ge(flo_made, T + l * 32 + g * 8 + (3, 4, 7, 8)[n])
                    unit(hu + 2 * CHUNKS, r + CHUNKS, f_hi, f_lo, gap_down)
                    with pe.Fori(1, CHUNKS) as c:
                        unit(hu + 2 * CHUNKS + c * 2, r + CHUNKS + c, f_hi, f_lo, no_gap)

                group(0, h_turns(l, 1))
                with pe.Fori(1, FF_GROUPS) as g:
                    group(g, no_gap)

        @block.scalar
        def _(act):
            def split_hi(hu, half, which=range(PAIRS)):
                for p in which:
                    act.wait_ge(raw_loaded[p], hu * 16 + 16)
                    act.wait_ge(w_used, hu * PAIRS + p + 1)
                    act.copy(w_hi[:, half * PAIRS + p, :], raw[:, p, :]).then_inc(hi_made, 1)

            def stationary_hi(i, dst, slot, k):
                act.wait_ge(xg_ready, i + 1)
                act.copy(dst, xg[:, slot, :].rearrange("p (k n) -> p k n", k=k)).then_inc(st_hi, 1)

            def h_chunks(l, h, which):
                for i in which:
                    t, c = H_ORDER[i]
                    stationary_hi(l * XG_LAYER + (0, XG_H2)[h] + i,
                                  h_hi[:, 4 * c:4 * c + 4, h_cols(t)], i % 2, 4)
                for i in which:
                    t, c = H_ORDER[i]
                    act.wait_ge(x_ready, l * 16 + 8 * h + i + 1)
                    if i:
                        act.wait_ge(sq_done, l * SQ_LAYER + (0, SQ_H2)[h] + i)
                    act.activation(junk[:, :], x[:, t, c_cols(c)], ACT.Square,
                                   accum_out=ss_x[:, t, c:c + 1]).then_inc(sq_done, 1)

            def take_proj(l, u):
                for t in range(T):
                    act.wait_ge(rstd_ready, T + l * RS_LAYER + RS_X1 + t + 1)
                    result_stands(act, t, l * ACC_LAYER + u, l * HU_LAYER + u * 2 + 1)
                    act.mul(proj_out(u, t), acc_bank[t][:, :], rstd[:, COL_X1 + t:COL_X1 + t + 1]
                            ).then_inc(acc_free[t], 1)

            def proj_out(u, t):
                if isinstance(u, int):
                    return proj[:, u, t, :]
                return proj[:, ld(u, 1), t, :].rearrange("p a c -> p (a c)")

            split_hi(0, 0)

            with act.Fori(0, DEPTH) as l:
                hu0 = l * HU_LAYER
                a0 = l * ACC_LAYER
                xg0 = l * XG_LAYER

                h_chunks(l, 0, (0, 1))
                h_chunks(l, 0, (2, 3))
                split_hi(hu0 + 1, 1)
                h_chunks(l, 0, (4, 5))
                h_chunks(l, 0, (6, 7))
                split_hi(hu0 + 2, 0)
                take_proj(l, 0)
                with act.Fori(1, 6) as u:
                    split_hi(hu0 + u * 2 + 1, 1)
                    split_hi(hu0 + u * 2 + 2, 0)
                    take_proj(l, u)

                with act.If(l < 1):
                    act.wait_ge(angle_ready, 1)
                    act.activation(sin_t[:, :, :], rt[0][:, :, :], ACT.Sin
                                   ).then_inc(rope_table_ready, 1)
                    act.activation(cos_t[:, :, :], rt[1][:, :, :], ACT.Sin
                                   ).then_inc(rope_table_ready, 1)

                def take_pooled(g):
                    act.wait_ge(pooled_done, l * 4 + g + 1)
                    act.copy(pooled_t[:, 2 * g:2 * g + 2, :],
                             s_bank[g % 2][:, :].rearrange("p (c n) -> p c n", c=2)
                             ).then_inc(pooled_ready, 1)

                split_hi(hu0 + 13, 1)
                for g in range(4):
                    take_pooled(g)
                split_hi(hu0 + 14, 0)
                take_proj(l, 6)

                split_hi(hu0 + 15, 1)
                act.wait_ge(y_ready, l * 4 + 4)
                for t in range(T):
                    act.wait_ge(sq_done, l * SQ_LAYER + SQ_Y + t)
                    act.activation(junk_y[:, :, :], y[:, :, t, :], ACT.Square,
                                   accum_out=ss_p[:, t:t + 1]).then_inc(sq_done, 1)
                for i in range(4):
                    t, c = Y_ORDER[i]
                    stationary_hi(xg0 + XG_Y + i,
                                  f_hi[:, 8 + 4 * c:12 + 4 * c, h_cols(t)], i % 2, 4)
                split_hi(hu0 + 16, 0)
                take_proj(l, 7)

                def take_probs_t(c):
                    for e in range(2):
                        act.wait_ge(tb_done[e], l * TB_LAYER + TB_QK + 2 * c + 2)
                        act.copy(probs_t[:, e, :, :],
                                 t_bank[e][:, :].rearrange("p (k n) -> p k n", k=2)
                                 ).then_inc(tb_free[e], 1)

                def take_heads(c):
                    act.wait_ge(o_done, l * 4 + c + 1)
                    if c > 0:
                        act.wait_ge(o_summed, l * 4 + c)
                    act.activation(o_sq[:, :], o_bank[:, :], ACT.Square).then_inc(o_squared, 1)
                    stationary_hi(xg0 + XG_O + c,
                                  f_hi[:, 2 * c:2 * c + 2, :], c % 2, 2)

                for c in range(CHUNKS):
                    hu, half = hu0 + HU_B1 + c, c % 2
                    if c > 0:
                        take_probs_t(c - 1)
                    for e in range(2):
                        act.wait_ge(tb_done[e], l * TB_LAYER + TB_QK + 2 * c + 1)
                        act.copy(qk_t[:, e, :], t_bank[e][:, :]).then_inc(tb_free[e], 1)
                    split_hi(hu + 1, 1 - half, (0, 1))
                    if c > 0:
                        take_heads(c - 1)
                    for e in range(2):
                        h = 2 * c + e
                        act.wait_ge(max_ready, l * HEADS + h + 1)
                        for t in range(T):
                            ex = act.activation(probs[:, e, t, :], probs[:, e, t, :], ACT.Exp,
                                                bias=neg_max[:, h, t:t + 1],
                                                accum_out=den[:, h, t:t + 1])
                            ex.then_inc(exp_done, 1)
                    split_hi(hu + 1, 1 - half, (2, 3))
                    for t in range(T):
                        act.wait_ge(rstd_ready, T + l * RS_LAYER + RS_P + 1)
                        result_stands(act, t, a0 + ACC_B1 + c, hu)
                        act.mul(acc[:, t, c_cols(c)], acc_bank[t][:, :],
                                rstd[:, COL_P + t:COL_P + t + 1]).then_inc(acc_free[t], 1)

                def post_squares(l, base, result, c):
                    for t in range(T):
                        act.wait_ge(acc_free[t], 1 + result + 1)
                        act.wait_ge(sq_done, l * SQ_LAYER + base + 2 * c + t)
                        act.activation(junk[:, :], acc_chunk(t, c), ACT.Square,
                                       accum_out=ss_chunk(t, c)).then_inc(sq_done, 1)

                def acc_chunk(t, c):
                    return acc[:, t, ld(c * CH, CH)]

                def ss_chunk(t, c):
                    return ss_post[:, t, ld(c, 1)]

                for c in range(CHUNKS):
                    hu, half = hu0 + HU_B2 + c, c % 2
                    if c == 0:
                        take_probs_t(CHUNKS - 1)
                        split_hi(hu + 1, 1 - half, (0, 1))
                        take_heads(CHUNKS - 1)
                        split_hi(hu + 1, 1 - half, (2, 3))
                    else:
                        split_hi(hu + 1, 1 - half)
                    post_squares(l, SQ_B2, a0 + ACC_B2 + c, c)

                def activate(g, u):
                    for t in range(T):
                        act.wait_ge(rstd_ready, T + l * RS_LAYER + RS_X2 + t + 1)
                        result_stands(act, t, a0 + ACC_F + g * 8 + u,
                                      hu0 + HU_F + g * HU_GROUP + u * 2 + 1)
                        act.activation(act_f[:, t, :], acc_bank[t][:, :], ACT.Relu,
                                       scale=rstd[:, COL_X2 + t:COL_X2 + t + 1]
                                       ).then_inc(acc_free[t], 1)
                        act.wait_ge(acc_free[t], 1 + a0 + ACC_F + g * 8 + u + 1)
                        act.activation(act_f[:, t, :], act_f[:, t, :], ACT.Square
                                       ).then_inc(f_ready, 1)

                def f_chunk_hi(g, u, t):
                    act.wait_ge(tb_done[t], l * TB_LAYER + TB_F + g * 4 + u + 1)
                    act.copy(f_out(f_hi, u, t), t_bank[t][:, :].rearrange("p (k n) -> p k n", k=4)
                             ).then_inc(fhi_made, 1)

                def group(g, first, last):
                    hu = hu0 + HU_F + g * HU_GROUP
                    if first:
                        h_chunks(l, 1, (0, 1))
                        h_chunks(l, 1, (2, 3))
                        split_hi(hu + 1, 1)
                        h_chunks(l, 1, (4, 5))
                        h_chunks(l, 1, (6, 7))
                    else:
                        split_hi(hu + 1, 1)
                    split_hi(hu + 2, 0)
                    activate(g, 0)
                    with act.Fori(1, CHUNKS) as u:
                        f_chunk_hi(g, u - 1, 0)
                        split_hi(hu + u * 2 + 1, 1)
                        f_chunk_hi(g, u - 1, 1)
                        split_hi(hu + u * 2 + 2, 0)
                        activate(g, u)
                    f_chunk_hi(g, CHUNKS - 1, 0)
                    split_hi(hu + 9, 1)
                    f_chunk_hi(g, CHUNKS - 1, 1)
                    split_hi(hu + 10, 0)
                    if not last:
                        with act.Fori(1, CHUNKS) as c:
                            split_hi(hu + 8 + c * 2 + 1, 1)
                            split_hi(hu + 8 + c * 2 + 2, 0)
                        return
                    r = a0 + ACC_F + g * 8 + CHUNKS
                    post_squares(l, SQ_F, r, 0)
                    with act.Fori(1, CHUNKS - 1) as c:
                        split_hi(hu + 8 + c * 2 + 1, 1)
                        split_hi(hu + 8 + c * 2 + 2, 0)
                        post_squares(l, SQ_F, r + c, c)
                    split_hi(hu + 15, 1)
                    with act.If(l < DEPTH - 1):
                        split_hi(hu + 16, 0)
                    post_squares(l, SQ_F, r + CHUNKS - 1, CHUNKS - 1)

                group(0, True, False)
                with act.Fori(1, FF_GROUPS - 1) as g:
                    group(g, False, False)
                group(FF_GROUPS - 1, False, True)

        @block.vector
        def _(dve):
            def split_lo(hu, half, which=range(PAIRS)):
                for p in which:
                    dve.wait_ge(hi_made, hu * PAIRS + p + 1)
                    slot = half * PAIRS + p
                    dve.tensor_tensor(w_lo[:, slot, :], raw[:, p, :],
                                      w_hi[:, slot, :].bitcast(F32), ALU.subtract
                                      ).then_inc(lo_made, 1)

            def scaled(i, slot, bank, g, k):
                dve.wait_ge(st_lo, i + 1)
                return dve.tensor_tensor(
                    xg[:, slot, :].rearrange("p (k n) -> p k n", k=k),
                    bank[:, :].rearrange("p (k n) -> p k n", k=k),
                    gain[:, g:g + k, None].to_broadcast([P, k, CH // k]), ALU.mult
                    ).then_inc(xg_ready, 1)

            def mean(col, src):
                dve.tensor_scalar(src, src, 1.0 / D, EPS, ALU.mult, ALU.add,
                                  accum_out=mean_sq[:, col:col + 1]).then_inc(mean_ready, 1)

            def add_post(l, h, i):
                t, c = H_ORDER[i]
                col = (COL_POST2, COL_POST1)[h] + t
                dve.wait_ge(rstd_ready, l * RS_LAYER + h * (RS_POST1 + T) + t + 1)
                dve.wait_ge(post_ready, l * 4 * CHUNKS + h * (2 * CHUNKS) + 2 * c + t + 1)
                dve.scalar_tensor_tensor(x[:, t, c_cols(c)], acc[:, t, c_cols(c)],
                                         rstd[:, col:col + 1], x[:, t, c_cols(c)],
                                         ALU.mult, ALU.add).then_inc(x_ready, 1)

            def h_chunks(l, h, which):
                for i in which:
                    add_post(l, h, i)
                for i in which:
                    t, c = H_ORDER[i]
                    dve.wait_ge(tb_done[i % 2], l * TB_LAYER + (0, TB_H2)[h] + i // 2 + 1)
                    scaled(l * XG_LAYER + (0, XG_H2)[h] + i, i % 2, t_bank[i % 2],
                           (G_MIX, G_FFN)[h] + 4 * c, 4)

            def mean_x(l, h):
                for t in range(T):
                    dve.wait_ge(sq_done, l * SQ_LAYER + (0, SQ_H2)[h] + 6 + 2 * t)
                    mean((COL_X1, COL_X2)[h] + t, ss_x[:, t, :])

            dve.sem_inc(lo_made, RAW)
            dve.sem_inc(flo_made, T)
            dve.memset(rstd[:, :], 1.0).then_inc(setup_done, 1)
            dve.memset(acc[:, 0, :], 0.0).then_inc(setup_done, 1)
            dve.memset(acc[:, 1, :], 0.0).then_inc(setup_done, 1)
            dve.memset(ones[:, :], 1.0).then_inc(setup_done, 1)
            dve.wait_ge(gains_turned, 1)
            dve.tensor_copy(gains[:, :], s_bank[0][:, 0:DEPTH * G_LAYER]).then_inc(gains_ready, 1)
            split_lo(0, 0)
            dve.wait_ge(setup_done, 4)
            dve.wait_ge(x_loaded, 16 * T)
            dve.wait_ge(gains_ready, 1)

            with dve.Fori(0, DEPTH) as l:
                hu0 = l * HU_LAYER
                a0 = l * ACC_LAYER
                xg0 = l * XG_LAYER

                dve.tensor_copy(gain[:, :], gains[:, ld(l * G_LAYER, G_LAYER)]
                                ).then_inc(gain_ready, 1)
                dve.wait_ge(gain_ready, l + 1)
                h_chunks(l, 0, (0, 1))
                h_chunks(l, 0, (2, 3))
                split_lo(hu0 + 1, 1)
                h_chunks(l, 0, (4, 5))
                h_chunks(l, 0, (6, 7))
                split_lo(hu0 + 2, 0)
                mean_x(l, 0)
                with dve.Fori(1, 6) as u:
                    split_lo(hu0 + u * 2 + 1, 1)
                    split_lo(hu0 + u * 2 + 2, 0)

                split_lo(hu0 + 13, 1)
                split_lo(hu0 + 14, 0)
                dve.wait_ge(scale_loaded, l * 16 + 16)
                for g in range(4):
                    dve.wait_ge(y_done, l * 4 + g + 1)
                    row = scale_row[:, g * GROUP:(g + 1) * GROUP]
                    dve.tensor_tensor(y[:, g // 2, :, (g % 2) * GROUP:(g % 2 + 1) * GROUP],
                                      s_bank[g % 2][:, :].rearrange("p (t n) -> p t n", t=T),
                                      row[:, None, :].to_broadcast([P, T, GROUP]), ALU.mult
                                      ).then_inc(y_ready, 1)

                split_lo(hu0 + 15, 1)
                for i in range(4):
                    t, c = Y_ORDER[i]
                    dve.wait_ge(tb_done[i % 2], l * TB_LAYER + TB_Y + i // 2 + 1)
                    scaled(xg0 + XG_Y + i, i % 2, t_bank[i % 2], G_POOL + 4 * c, 4
                           )
                for t in range(T):
                    dve.wait_ge(sq_done, l * SQ_LAYER + SQ_Y + t + 1)
                dve.tensor_scalar(mean_sq[:, COL_P:COL_P + 2], ss_p[:, :], 1.0 / HALF_W, EPS,
                                  ALU.mult, ALU.add).then_inc(mean_ready, 1)
                split_lo(hu0 + 16, 0)

                dve.wait_ge(rope_table_ready, 2)
                dve.wait_ge(st_lo, xg0 + XG_O + XG_SLOTS)
                hr = ROPE // 2
                for t in range(T):
                    dve.wait_ge(acc_free[t], 1 + a0 + 6)
                    qk = proj[:, 2:6, t, :].rearrange("p u (h d) -> p u h d", d=P)
                    x1, x2 = qk[:, :, :, 0:hr], qk[:, :, :, hr:ROPE]
                    cs = cos_t[:, t, None, None, :].to_broadcast([P, 4, 4, hr])
                    sn = sin_t[:, t, None, None, :].to_broadcast([P, 4, 4, hr])
                    step = l * 12 + t * 6
                    if t:
                        dve.wait_ge(rope_step, step)
                    for n, (a, b) in enumerate(((x1, cs), (x2, sn), (x2, cs), (x1, sn))):
                        dve.tensor_tensor(rope_tmp[:, n], a, b, ALU.mult).then_inc(rope_step, 1)
                    dve.wait_ge(rope_step, step + 4)
                    dve.tensor_tensor(x1, rope_tmp[:, 0], rope_tmp[:, 1], ALU.subtract
                                      ).then_inc(rope_step, 1)
                    dve.tensor_tensor(x2, rope_tmp[:, 2], rope_tmp[:, 3], ALU.add
                                      ).then_inc(rope_step, 1)
                dve.wait_ge(rope_step, l * 12 + 12)

                def take_heads(c):
                    dve.wait_ge(o_squared, l * 4 + c + 1)
                    scaled(xg0 + XG_O + c, c % 2, o_bank, G_ATTN + 2 * c, 2)
                    if c == 0:
                        dve.tensor_copy(o_sqsum[:, :], o_sq[:, :]).then_inc(o_summed, 1)
                    else:
                        dve.wait_ge(o_summed, l * 4 + c)
                        dve.tensor_tensor(o_sqsum[:, :], o_sqsum[:, :], o_sq[:, :], ALU.add
                                          ).then_inc(o_summed, 1)

                for c in range(CHUNKS):
                    hu, half = hu0 + HU_B1 + c, c % 2
                    split_lo(hu + 1, 1 - half, (0, 1))
                    if c > 0:
                        take_heads(c - 1)
                    if c == 0:
                        dve.wait_ge(bias_ready, 1)
                    for e in range(2):
                        h = 2 * c + e
                        dve.wait_ge(s_done, l * HEADS + h + 1)
                        if c > 0:
                            dve.wait_ge(tb_done[e], l * TB_LAYER + TB_QK + 2 * c)
                        dve.scalar_tensor_tensor(
                            probs[:, e].rearrange("p t n -> p (t n)"), s_bank[e][:, :],
                            float(P) ** -0.5, bias[:, :, :].rearrange("p t n -> p (t n)"),
                            ALU.mult, ALU.add).then_inc(score_ready, 1)
                        dve.wait_ge(score_ready, l * HEADS + h + 1)
                        dve.tensor_reduce(neg_max[:, h, :], probs[:, e, :, :], AX.X, ALU.max,
                                          negate=True).then_inc(max_ready, 1)
                    for e in range(2):
                        h = 2 * c + e
                        dve.wait_ge(exp_done, l * 2 * HEADS + 2 * h + 2)
                        dve.reciprocal(rden[:, h, :], den[:, h, :]).then_inc(rden_ready, 1)
                        dve.wait_ge(rden_ready, l * HEADS + h + 1)
                        dve.tensor_scalar(probs[:, e, 0, :], probs[:, e, 0, :], rden[:, h, 0:1],
                                          None, ALU.mult)
                        dve.tensor_scalar(probs[:, e, 1, :], probs[:, e, 1, :], rden[:, h, 1:2],
                                          None, ALU.mult).then_inc(prob_ready, 1)
                    split_lo(hu + 1, 1 - half, (2, 3))

                def mixed(c):
                    for t in range(T):
                        dve.wait_ge(rstd_ready, T + l * RS_LAYER + RS_A + 1)
                        result_stands(dve, t, a0 + ACC_B2 + c, hu0 + HU_B2 + c)
                        dve.scalar_tensor_tensor(acc[:, t, c_cols(c)], acc_bank[t][:, :],
                                                 rstd[:, COL_A + t:COL_A + t + 1],
                                                 acc[:, t, c_cols(c)], ALU.mult, ALU.add
                                                 ).then_inc(acc_free[t], 1)
                        if c == CHUNKS - 1:
                            dve.wait_ge(sq_done, l * SQ_LAYER + SQ_B2 + 2 * c + t + 1)
                            mean(COL_POST1 + t, ss_post[:, t, :])

                for c in range(CHUNKS):
                    hu, half = hu0 + HU_B2 + c, c % 2
                    if c == 0:
                        split_lo(hu + 1, 1 - half, (0, 1))
                        take_heads(CHUNKS - 1)
                        split_lo(hu + 1, 1 - half, (2, 3))
                        dve.wait_ge(ssa_done, l + 1)
                        dve.tensor_scalar(mean_sq[:, COL_A:COL_A + 2], ssa_bank[:, 0:2],
                                          1.0 / HALF_W, EPS, ALU.mult, ALU.add
                                          ).then_inc(mean_ready, 1)
                    else:
                        split_lo(hu + 1, 1 - half)
                    mixed(c)

                def f_chunk_lo(g, u, t):
                    dve.wait_ge(fhi_made, l * 32 + g * 8 + u * 2 + t + 1)
                    dve.tensor_tensor(f_out(f_lo, u, t),
                                      t_bank[t][:, :].rearrange("p (k n) -> p k n", k=4),
                                      f_out(f_hi, u, t).bitcast(F32), ALU.subtract
                                      ).then_inc(flo_made, 1)

                def down_sum(g, c, first):
                    for t in range(T):
                        result_stands(dve, t, a0 + ACC_F + g * 8 + CHUNKS + c,
                                      hu0 + HU_F + g * HU_GROUP + 2 * CHUNKS + c * 2 + 1)
                        dst = acc[:, t, ld(c * CH, CH)]
                        if first:
                            dve.tensor_copy(dst, acc_bank[t][:, :]).then_inc(acc_free[t], 1)
                        else:
                            dve.tensor_tensor(dst, acc_bank[t][:, :], dst, ALU.add
                                              ).then_inc(acc_free[t], 1)

                def group(g, first, last):
                    hu = hu0 + HU_F + g * HU_GROUP
                    if first:
                        h_chunks(l, 1, (0, 1))
                        h_chunks(l, 1, (2, 3))
                        split_lo(hu + 1, 1)
                        h_chunks(l, 1, (4, 5))
                        h_chunks(l, 1, (6, 7))
                        split_lo(hu + 2, 0)
                        mean_x(l, 1)
                    else:
                        split_lo(hu + 1, 1)
                        split_lo(hu + 2, 0)
                    with dve.Fori(1, CHUNKS) as u:
                        f_chunk_lo(g, u - 1, 0)
                        split_lo(hu + u * 2 + 1, 1)
                        f_chunk_lo(g, u - 1, 1)
                        split_lo(hu + u * 2 + 2, 0)
                    f_chunk_lo(g, CHUNKS - 1, 0)
                    split_lo(hu + 9, 1)
                    f_chunk_lo(g, CHUNKS - 1, 1)
                    split_lo(hu + 10, 0)
                    down_sum(g, 0, first)
                    with dve.Fori(1, CHUNKS - 1) as c:
                        split_lo(hu + 8 + c * 2 + 1, 1)
                        split_lo(hu + 8 + c * 2 + 2, 0)
                        down_sum(g, c, first)
                    split_lo(hu + 15, 1)
                    if last:
                        with dve.If(l < DEPTH - 1):
                            split_lo(hu + 16, 0)
                    else:
                        split_lo(hu + 16, 0)
                    down_sum(g, CHUNKS - 1, first)
                    if last:
                        for t in range(T):
                            dve.wait_ge(sq_done, l * SQ_LAYER + SQ_F + 2 * (CHUNKS - 1) + t + 1)
                            mean(COL_POST2 + t, ss_post[:, t, :])

                group(0, True, False)
                with dve.Fori(1, FF_GROUPS - 1) as g:
                    group(g, False, False)
                group(FF_GROUPS - 1, False, True)

            for i in range(2 * CHUNKS):
                add_post(DEPTH, 0, i)


        @block.gpsimd
        def _(pool):
            def stationary_lo(i, hi, lo, slot, k):
                pool.wait_ge(st_hi, i + 1)
                pool.tensor_tensor(lo, xg[:, slot, :].rearrange("p (k n) -> p k n", k=k),
                                   hi.bitcast(F32), ALU.subtract).then_inc(st_lo, 1)

            def h_chunks(l, h):
                for i, (t, c) in enumerate(H_ORDER):
                    stationary_lo(l * XG_LAYER + (0, XG_H2)[h] + i,
                                  h_hi[:, 4 * c:4 * c + 4, h_cols(t)],
                                  h_lo[:, 4 * c:4 * c + 4, h_cols(t)], i % 2, 4)

            def root(l, rs, col, n=1):
                pool.wait_ge(mean_ready, l * RS_LAYER + rs + 1)
                pool.tensor_tensor(rstd[:, col:col + n], mean_sq[:, col:col + n],
                                   minus_half[:, 0:n], ALU.pow).then_inc(rstd_ready, 1)

            def post_gain(l, h, t, c):
                pool.wait_ge(sq_done, l * SQ_LAYER + (SQ_B2, SQ_F)[h] + 2 * c + t + 1)
                part = acc[:, t, ld(c * CH, CH)]
                pool.tensor_tensor(part, part, post_row[:, ld(c * CH, CH)], ALU.mult
                                   ).then_inc(post_ready, 1)

            def post_gains(l, h, rs, col):
                pool.wait_ge(post_row_loaded, l * 32 + 16 * h + 16)
                for c in range(CHUNKS - 1):
                    for t in range(T):
                        post_gain(l, h, t, c)
                for t in range(T):
                    root(l, rs + t, col + t)
                    post_gain(l, h, t, CHUNKS - 1)

            pool.sem_inc(st_lo, XG_SLOTS)
            pool.sem_inc(rstd_ready, T)
            pool.sem_inc(post_ready, T_INIT)
            pool.memset(ident[:, :], 0.0).then_inc(ident_made, 1)
            pool.memset(minus_half[:, :], -0.5).then_inc(table_step, 1)
            pool.wait_ge(ident_made, 1)
            pool.affine_select(ident[:, :], ident[:, :], [[-1, P]], ALU.not_equal, 1.0, base=0,
                               channel_multiplier=1).then_inc(ident_made, 1)
            pool.wait_ge(table_step, 1)

            steps = [1]

            def step(ins):
                steps[0] += 1
                ins.then_inc(table_step, 1)
                pool.wait_ge(table_step, steps[0])

            def rope_tables():
                ang, theta_c, r, turns, p1, p2 = (a[:, :, :] for a in rt)
                q = rt_i[:, :, :]
                half = ROPE // 2
                inv = (THETA ** (-np.arange(0, ROPE, 2, dtype=np.float64) / ROPE)).astype(np.float32)
                for n in range(half):
                    step(pool.memset(freq[:, n:n + 1], float(inv[n])))
                pool.wait_ge(pos_loaded, 16)
                step(pool.tensor_copy(pos_f[:, :], pos_i[:, :]))
                for t in range(T):
                    step(pool.tensor_scalar(rt[2][:, t, :], freq[:, :], pos_f[:, t:t + 1], None,
                                            ALU.mult))
                step(pool.memset(turns, 0.0))
                for unit in (2.0 ** 20, 2.0 ** 9):
                    step(pool.tensor_scalar(q, r, 1.0 / unit, None, ALU.mult))
                    step(pool.tensor_copy(p1, q))
                    step(pool.tensor_scalar(p2, p1, unit, None, ALU.mult))
                    step(pool.tensor_tensor(r, r, p2, ALU.subtract))
                    whole = unit / (2 * np.pi)
                    part = whole - round(whole)
                    c1 = trunc_bits(part, 12)
                    c2 = trunc_bits(part - c1, 12)
                    c3 = part - c1 - c2
                    step(pool.tensor_scalar(p2, p1, c1, None, ALU.mult))
                    step(pool.tensor_copy(q, p2))
                    step(pool.tensor_copy(ang, q))
                    step(pool.tensor_tensor(p2, p2, ang, ALU.subtract))
                    step(pool.tensor_tensor(turns, turns, p2, ALU.add))
                    for part in (c2, c3):
                        step(pool.tensor_scalar(p2, p1, float(part), None, ALU.mult))
                        step(pool.tensor_tensor(turns, turns, p2, ALU.add))
                step(pool.tensor_scalar(p1, r, float(1 / (2 * np.pi)), None, ALU.mult))
                step(pool.tensor_tensor(p1, p1, turns, ALU.add))
                step(pool.tensor_copy(q, p1))
                step(pool.tensor_copy(p1, q))
                c1 = trunc_bits(2 * np.pi, 16)
                c2 = trunc_bits(2 * np.pi - c1, 16)
                for part in (c1, c2, 2 * np.pi - c1 - c2):
                    step(pool.tensor_scalar(p2, p1, float(part), None, ALU.mult))
                    step(pool.tensor_tensor(r, r, p2, ALU.subtract))
                step(pool.tensor_scalar(p2, turns, float(2 * np.pi), None, ALU.mult))
                step(pool.tensor_tensor(r, r, p2, ALU.add))
                step(pool.tensor_scalar(ang, r, 3.1415925, -3.1415925, ALU.min, ALU.max))
                step(pool.tensor_scalar(p1, ang, 0.0, None, ALU.max))
                step(pool.tensor_scalar(p2, ang, 0.0, None, ALU.min))
                step(pool.tensor_tensor(p1, p1, p2, ALU.subtract))
                pool.tensor_scalar(theta_c, p1, -1.0, float(np.pi / 2), ALU.mult, ALU.add
                                   ).then_inc(angle_ready, 1)

            def bias_table():
                b = bias[:, :, :]
                d, m, c = (a[:, :, :] for a in tmp)
                step(pool.iota(tmp_i[:, :, :], [[-P, T], [1, SEQ]], base=SEQ, channel_multiplier=-1))
                step(pool.tensor_copy(d, tmp_i[:, :, :]))
                step(pool.tensor_scalar(m, d, float(SEQ - 64), None, ALU.is_ge))
                step(pool.tensor_scalar(c, d, float(SEQ + 64), None, ALU.is_le))
                step(pool.tensor_tensor(c, c, m, ALU.mult))
                for dilation in (4, 16):
                    step(pool.tensor_scalar(tmp_i[:, :, :], d, 1.0 / dilation,
                                            -(dilation - 1) / (2.0 * dilation), ALU.mult, ALU.add))
                    step(pool.tensor_copy(m, tmp_i[:, :, :]))
                    step(pool.tensor_scalar(m, m, float(dilation), None, ALU.mult))
                    step(pool.tensor_tensor(m, d, m, ALU.subtract))
                    step(pool.tensor_scalar(m, m, 0.0, None, ALU.is_equal))
                    step(pool.tensor_tensor(c, c, m, ALU.add))
                step(pool.tensor_scalar(b, c, 0.0, NEG_BIG, ALU.is_equal, ALU.mult))
                for n in (2, 3):
                    step(pool.tensor_scalar(m, c, float(n), float(np.log(n)), ALU.is_equal,
                                            ALU.mult))
                    step(pool.tensor_tensor(b, b, m, ALU.add))
                pool.sem_inc(bias_ready, 1)

            def band_table():
                eye = tmp[0][:, :, 0:BAND]
                row = tmp[1][:, 0, :]
                step(pool.memset(eye, 0.0))
                step(pool.affine_select(eye, eye, [[BAND_AT - P, T], [1, BAND]], ALU.not_equal, 1.0,
                                        base=0, channel_multiplier=-1))
                for n, w in enumerate(WINDOWS):
                    h = w // 2
                    step(pool.memset(row, 1.0 / w))
                    for i in range(h):
                        step(pool.memset(row[:, i:i + 1], 1.0 / (i + h)))
                    for i in range(SEQ - h + 1, SEQ):
                        step(pool.memset(row[:, i:i + 1], 1.0 / (SEQ - i + h)))
                    for jt in range(T):
                        b = band[:, n, jt, :]
                        at_i = jt * (BAND_AT - P)
                        step(pool.affine_select(b, row[:, jt * BAND_AT:jt * BAND_AT + BAND],
                                                [[-1, BAND]], ALU.is_ge, 0.0, base=h - at_i,
                                                channel_multiplier=1))
                        step(pool.affine_select(b, b, [[1, BAND]], ALU.is_ge, 0.0,
                                                base=at_i + h - 1, channel_multiplier=-1))
                        step(pool.tensor_tensor(b, b, eye[:, jt, :], ALU.subtract))
                pool.sem_inc(band_ready, 1)

            with pool.Fori(0, DEPTH) as l:
                xg0 = l * XG_LAYER
                h_chunks(l, 0)
                root(l, RS_X1, COL_X1)
                root(l, RS_X1 + 1, COL_X1 + 1)
                with pool.If(l < 1):
                    rope_tables()
                    bias_table()
                    band_table()
                for i in range(4):
                    t, c = Y_ORDER[i]
                    stationary_lo(xg0 + XG_Y + i, f_hi[:, 8 + 4 * c:12 + 4 * c, h_cols(t)],
                                  f_lo[:, 8 + 4 * c:12 + 4 * c, h_cols(t)], i % 2, 4)
                root(l, RS_P, COL_P, 2)
                for c in range(CHUNKS):
                    stationary_lo(xg0 + XG_O + c, f_hi[:, 2 * c:2 * c + 2, :],
                                  f_lo[:, 2 * c:2 * c + 2, :], c % 2, 2)
                root(l, RS_A, COL_A, 2)
                post_gains(l, 0, RS_POST1, COL_POST1)
                h_chunks(l, 1)
                root(l, RS_X2, COL_X2)
                root(l, RS_X2 + 1, COL_X2 + 1)
                post_gains(l, 1, RS_POST2, COL_POST2)


_INS = ("x", "positions", "g_mix_pre", "w_in", "g_attn_out", "w_pool", "pool_scale", "g_pool_out",
        "w_out", "g_mix_post", "g_ffn_pre", "w_up", "w_down", "g_ffn_post")


def kernel(**inputs):
    import concourse.bacc as bacc
    from concourse.bass_utils import run_bass_kernel_spmd

    nc = bacc.Bacc("TRN2", target_bir_lowering=False, num_devices=1, dynamic_dma_scratch_size=1024)
    arrays, args = {}, []
    for name in _INS:
        a = np.ascontiguousarray(inputs[name])
        arrays[f"in_{name}"] = a
        args.append(nc.dram_tensor(f"in_{name}", a.shape, mybir.dt.from_np(a.dtype),
                                   kind="ExternalInput").ap())
    out = nc.dram_tensor("out", (1, SEQ, D), F32, kind="ExternalOutput").ap()
    build(nc, *args, out)
    r = run_bass_kernel_spmd(nc, [arrays], core_ids=[0])
    return r.results[0]["out"]
```

```python
import numpy as np

import concourse.bass as bass
from concourse import mybir

F32 = mybir.dt.float32
F32R = mybir.dt.float32r
I32 = mybir.dt.int32
ALU = mybir.AluOpType
ACT = mybir.ActivationFunctionType
AX = mybir.AxisListType

P = 128
D = 2048
SEQ = 256
DEPTH = 2
T = SEQ // P
HALF_W = D // 2
HEADS = HALF_W // 128
WINDOWS = (2, 4, 8, 16)
GROUP = HALF_W // len(WINDOWS)
D_FF = 4 * D
ROPE = 32
THETA = 500000.0
EPS = 1e-6
NEG_BIG = -1e30
CH = 512
KT = D // P
PAIRS = 4
FF_GROUPS = D_FF // D
UNITS_A = 8
CHUNKS = D // CH

HU_B1 = 2 * UNITS_A
HU_B2 = HU_B1 + CHUNKS
HU_F = HU_B2 + CHUNKS
HU_GROUP = 4 * CHUNKS
HU_LAYER = HU_F + FF_GROUPS * HU_GROUP

ACC_B1 = UNITS_A
ACC_B2 = ACC_B1 + CHUNKS
ACC_F = ACC_B2 + CHUNKS
ACC_LAYER = ACC_F + FF_GROUPS * 2 * CHUNKS

TB_Y = 4
TB_QK = 6
TB_H2 = 14
TB_F = 18
TB_LAYER = TB_F + FF_GROUPS * CHUNKS

XG_Y = 8
XG_O = 12
XG_H2 = 16
XG_LAYER = 24

SQ_Y = 8
SQ_B2 = 10
SQ_H2 = 18
SQ_F = 26
SQ_LAYER = 34
RS_X1, RS_P, RS_A, RS_POST1, RS_X2, RS_POST2 = 0, 2, 3, 4, 6, 8
RS_LAYER = 10
COL_X1, COL_P, COL_A, COL_POST1, COL_X2, COL_POST2 = 0, 2, 4, 6, 8, 10

G_MIX, G_FFN, G_ATTN, G_POOL, G_LAYER = 0, 16, 32, 40, 48

Y_ORDER = [(0, 0), (1, 0), (0, 1), (1, 1)]


def mix_order(t, c):
    return 4 * (c // 2) + 2 * t + c % 2


def ff_order(t, c):
    return 2 * c + t


BAND = P + max(WINDOWS) // 2
BAND_AT = SEQ - BAND

RING = 2 * PAIRS
RAW = PAIRS
XG_SLOTS = 2
T_INIT = 2 * CHUNKS


def trunc_bits(v, bits):
    m, e = np.frexp(v)
    return float(np.ldexp(np.trunc(np.ldexp(m, bits)), int(e) - bits))


def build(nc, x_in, positions, g_mix_pre, w_in, g_attn_out, w_pool, pool_scale, g_pool_out,
          w_out, g_mix_post, g_ffn_pre, w_up, w_down, g_ffn_post, out):
    top = [((nc.sbuf_base + 31) // 32) * 32]

    def region(nbytes):
        at = top[0]
        top[0] += (nbytes + 31) // 32 * 32
        assert top[0] <= nc.sbuf_usable_end, top[0]
        return at

    def at(name, shape, dtype, offset):
        return nc.alloc_sbuf_tensor_at(name, shape, dtype, offset=offset)

    def own(name, shape, dtype=F32):
        return at(name, shape, dtype, region(4 * int(np.prod(shape[1:]))))

    x = own("x", [P, T, D])
    raw = own("raw", [P, RAW, 2 * CH])
    w_hi = own("w_hi", [P, RING, 2 * CH], F32R)
    w_lo = own("w_lo", [P, RING, 2 * CH], F32R)
    r_h = region(2 * 4 * KT * SEQ)
    h_hi = at("h_hi", [P, KT, SEQ], F32R, r_h)
    h_lo = at("h_lo", [P, KT, SEQ], F32R, r_h + 4 * KT * SEQ)
    qk_t = at("qk_t", [P, 2, 2 * SEQ], F32, r_h)
    probs = at("probs", [P, 2, T, SEQ], F32, r_h + 4096)
    probs_t = at("probs_t", [P, 2, T, SEQ], F32, r_h + 8192)
    o_sq = at("o_sq", [P, 2 * SEQ], F32, r_h + 12288)
    o_sqsum = at("o_sqsum", [P, 2 * SEQ], F32, r_h + 14336)
    r_f = region(2 * 4 * KT * SEQ)
    f_hi = at("f_hi", [P, KT, SEQ], F32R, r_f)
    f_lo = at("f_lo", [P, KT, SEQ], F32R, r_f + 4 * KT * SEQ)
    w_pool_s = at("w_pool_s", [P, len(WINDOWS) * 2, GROUP], F32, r_f)
    scale_row = at("scale_row", [P, HALF_W], F32, r_f + 4 * KT * SEQ)
    r_acc = region(4 * T * D)
    acc = at("acc", [P, T, D], F32, r_acc)
    pooled_t = at("pooled_t", [P, 2 * len(WINDOWS), SEQ], F32, r_acc)
    tmp_i = at("tmp_i", [P, T, SEQ], I32, r_acc)
    tmp = [at(f"tmp{n}", [P, T, SEQ], F32, r_acc + 2048 * (n + 1)) for n in range(3)]
    r_qkv = region(4 * 6 * T * CH)
    assert r_qkv == r_acc + 4 * T * D
    proj = at("proj", [P, UNITS_A, T, CH], F32, r_acc + 4 * D)
    y = at("y", [P, 2, T, CH], F32, r_acc + 4 * D)
    junk = at("junk", [P, CH], F32, r_qkv + 4 * T * CH)
    junk_y = at("junk_y", [P, 2, CH], F32, r_acc)
    act_f = at("act_f", [P, T, CH], F32, r_qkv)
    post_row = own("post_row", [P, D])
    r_xg = region(4 * XG_SLOTS * CH)
    xg = at("xg", [P, XG_SLOTS, CH], F32, r_xg)
    rope_tmp = at("rope_tmp", [P, 4, 4, 4, ROPE // 2], F32, r_xg)
    ident = own("ident", [P, P])
    bias = own("bias", [P, T, SEQ])
    band = own("band", [P, len(WINDOWS), T, BAND])
    rows_mix = at("rows_mix", [2 * KT, P], F32, r_f)
    rows_others = at("rows_others", [4 * KT, P], F32, r_f + 4 * P)
    gains_d = own("gains_d", [P, 2, DEPTH + 1, KT])
    gains_half = own("gains_half", [P, 2, DEPTH + 1, KT // 2])
    gain = own("gain", [P, G_LAYER])
    cos_t = own("cos_t", [P, T, ROPE // 2])
    sin_t = own("sin_t", [P, T, ROPE // 2])
    pos_i = own("pos_i", [P, T], I32)
    ss_x = own("ss_x", [P, T, CHUNKS])
    ss_post = own("ss_post", [P, T, CHUNKS])
    ss_p = own("ss_p", [P, T])
    mean_sq = own("mean_sq", [P, 12])
    rstd = own("rstd", [P, 12])
    neg_max = own("neg_max", [P, HEADS, T])
    den = own("den", [P, HEADS, T])
    rden = own("rden", [P, HEADS, T])
    minus_half = own("minus_half", [P, 2])
    ones = own("ones", [P, 1])
    warm = own("warm", [P, 1])
    rt = [own(f"rt{n}", [P, T, ROPE // 2]) for n in range(6)]
    rt_i = own("rt_i", [P, T, ROPE // 2], I32)
    pos_f = own("pos_f", [P, T])
    freq = own("freq", [P, ROPE // 2])

    acc_bank = [nc.alloc_psum_tensor(f"acc_bank{t}", [P, CH], F32) for t in range(T)]
    t_bank = [nc.alloc_psum_tensor(f"t_bank{n}", [P, CH], F32) for n in range(2)]
    s_bank = [nc.alloc_psum_tensor(f"s_bank{n}", [P, CH], F32) for n in range(2)]
    o_bank = nc.alloc_psum_tensor("o_bank", [P, CH], F32)
    ssa_bank = nc.alloc_psum_tensor("ssa_bank", [P, CH], F32)

    sem = nc.alloc_semaphore
    gains_loaded, others_loaded, pos_loaded = (sem("gains_loaded"), sem("others_loaded"),
                                               sem("pos_loaded"))
    ones_made, warm_done = sem("ones_made"), sem("warm_done")
    x_loaded = [sem(f"x_loaded{n}") for n in range(3)]
    raw_loaded = [sem(f"raw_loaded{p}") for p in range(RAW)]
    pool_w_loaded, scale_loaded = sem("pool_w_loaded"), sem("scale_loaded")
    post_row_loaded = sem("post_row_loaded")
    stored = sem("stored")
    hi_made, lo_made, w_used = sem("hi_made"), sem("lo_made"), sem("w_used")
    acc_done = sem("acc_done")
    acc_free = [sem(f"acc_free{t}") for t in range(T)]
    tb_done = [sem(f"tb_done{n}") for n in range(2)]
    tb_free = [sem(f"tb_free{n}") for n in range(2)]
    x_ready, xg_ready = sem("x_ready"), sem("xg_ready")
    st_hi, st_lo = sem("st_hi"), sem("st_lo")
    sq_done, mean_ready, rstd_ready = sem("sq_done"), sem("mean_ready"), sem("rstd_ready")
    post_ready = sem("post_ready")
    f_ready, fhi_made, flo_made = sem("f_ready"), sem("fhi_made"), sem("flo_made")
    setup_done, gains_turned, gains_ready, gain_ready = (sem("setup_done"), sem("gains_turned"),
                                                         sem("gains_ready"), sem("gain_ready"))
    ident_made, table_step, band_ready, bias_ready = (sem("ident_made"), sem("table_step"),
                                                      sem("band_ready"), sem("bias_ready"))
    angle_ready, rope_table_ready = sem("angle_ready"), sem("rope_table_ready")
    pooled_done, pooled_ready, y_done, y_ready = (sem("pooled_done"), sem("pooled_ready"),
                                                  sem("y_done"), sem("y_ready"))
    rope_step = sem("rope_step")
    s_done, score_ready, max_ready = sem("s_done"), sem("score_ready"), sem("max_ready")
    exp_done, rden_ready, prob_ready = sem("exp_done"), sem("rden_ready"), sem("prob_ready")
    o_done, o_squared, o_summed = sem("o_done"), sem("o_squared"), sem("o_summed")
    ssa_done = sem("ssa_done")

    def h_cols(t):
        return slice(t * P, (t + 1) * P)

    def c_cols(c):
        return slice(c * CH, (c + 1) * CH)

    ld = bass.ds

    def f_out(dst, u, t):
        return dst[:, ld(u * 4, 4), h_cols(t)]

    def result_stands(eng, t, result, hu):
        if t == 0:
            eng.wait_ge(acc_done, result + 1)
        else:
            eng.wait_ge(w_used, RING + PAIRS * hu + PAIRS)

    with nc.Block() as block:

        @block.sync
        def _(sp):
            sp.dma_start(rows_mix[:, :], g_mix_pre.rearrange("l (k p) -> (l k) p", p=P)
                         ).then_inc(gains_loaded, 16)
            x_rows = x_in[0].rearrange("(t p) d -> t p d", p=P)
            sp.dma_start(x[:, 0, 0:D // 2], x_rows[0][:, 0:D // 2]).then_inc(x_loaded[0], 16)

            def load_half(w, l, row, col, hu):
                for p in range(PAIRS):
                    sp.wait_ge(lo_made, hu * PAIRS + p + 1)
                    src = w[ld(l, 1), ld(row + p * 2 * P, 2 * P), ld(col, CH)]
                    sp.dma_start(raw[:, p, :].rearrange("p (k c) -> p k c", k=2),
                                 src.rearrange("a (k p) c -> p (a k) c", p=P)
                                 ).then_inc(raw_loaded[p], 16)

            def load_unit(w, l, row, col, hu):
                load_half(w, l, row, col, hu)
                load_half(w, l, row + HALF_W, col, hu + 1)

            def load_post_row(g, l):
                src = g[ld(l, 1), :].to_broadcast([P, D])
                sp.dma_start(post_row[:, :], src).then_inc(post_row_loaded, 16)

            def load_group(l, g):
                hu = l * HU_LAYER + HU_F + g * HU_GROUP
                with sp.Fori(0, CHUNKS) as u:
                    load_unit(w_up, l, 0, g * D + u * CH, hu + u * 2)
                with sp.Fori(0, CHUNKS) as c:
                    load_unit(w_down, l, g * D, c * CH, hu + 2 * CHUNKS + c * 2)

            with sp.Fori(0, DEPTH) as l:
                hu = l * HU_LAYER
                with sp.Fori(0, 2) as u:
                    load_unit(w_in, l, 0, 3 * HALF_W + u * CH, hu + u * 2)
                sp.wait_ge(acc_done, l * ACC_LAYER + 1)
                sp.dma_start(w_pool_s[:, :, :],
                             w_pool[ld(l, 1)].rearrange("a g (c p) d -> p (a g c) d", p=P)
                             ).then_inc(pool_w_loaded, 16)
                sp.dma_start(scale_row[:, :], pool_scale[ld(l, 1), :].to_broadcast([P, HALF_W])
                             ).then_inc(scale_loaded, 16)
                with sp.Fori(0, 6) as u:
                    load_unit(w_in, l, 0, u * CH, hu + 4 + u * 2)
                sp.wait_ge(post_ready, T_INIT + l * 4 * CHUNKS)
                load_post_row(g_mix_post, l)
                with sp.Fori(0, CHUNKS) as c:
                    load_half(w_out, l, HALF_W, c * CH, hu + HU_B1 + c)
                with sp.Fori(0, CHUNKS) as c:
                    load_half(w_out, l, 0, c * CH, hu + HU_B2 + c)
                with sp.Fori(0, FF_GROUPS - 1) as g:
                    load_group(l, g)
                sp.wait_ge(post_ready, T_INIT + l * 4 * CHUNKS + 2 * CHUNKS)
                load_post_row(g_ffn_post, l)
                load_group(l, FF_GROUPS - 1)

            out_rows = out[0].rearrange("(t p) d -> t p d", p=P)
            for t in range(T):
                for c in range(CHUNKS):
                    sp.wait_ge(x_ready, 16 * DEPTH + t * CHUNKS + c + 1)
                    sp.dma_start(out_rows[t][:, c_cols(c)], x[:, t, c_cols(c)]).then_inc(stored, 16)
            sp.wait_ge(stored, 16 * T * CHUNKS)

        @block.tensor
        def _(pe):
            def pair(t, p, hu, half, hi, lo, k0, bank, first, last, result):
                slot = half * PAIRS + p
                begin, end = first and p == 0, last and p == PAIRS - 1
                if begin:
                    pe.wait_ge(acc_free[t], result + 1)
                if t == 0:
                    pe.wait_ge(lo_made, hu * PAIRS + p + 1 + RAW)
                for k in range(2):
                    kt = k0 + 2 * p + k
                    xh, xl = hi[:, kt, h_cols(t)], lo[:, kt, h_cols(t)]
                    wh = w_hi[:, slot, c_cols(k)]
                    wl = w_lo[:, slot, c_cols(k)]
                    pe.matmul(bank[:, :], xh, wh, start=begin and k == 0, stop=False)
                    pe.matmul(bank[:, :], xh, wl, start=False, stop=False)
                    mm = pe.matmul(bank[:, :], xl, wh, start=False, stop=end and k == 1)
                if t == 1:
                    mm.then_inc(w_used, 1)
                elif end:
                    mm.then_inc(acc_done, 1)

            def unit(hu, result, hi, lo, before=None):
                for n in range(4):
                    t, half = n // 2, n % 2
                    for p in range(PAIRS):
                        if before is not None:
                            before(n, p)
                        pair(t, p, hu + half, half, hi, lo, 8 * half, acc_bank[t],
                             half == 0, half == 1, result)

            def h_turns(l, h, which):
                for i in which:
                    t, c = i // CHUNKS, i % CHUNKS
                    pe.wait_ge(x_ready, l * 16 + 8 * h + i + 1)
                    if i >= 2:
                        pe.wait_ge(xg_ready, l * XG_LAYER + (0, XG_H2)[h] + i - 1)
                    for j in range(4):
                        tr = pe.transpose(t_bank[i % 2][:, h_cols(j)],
                                          x[:, t, c * CH + j * P:c * CH + (j + 1) * P],
                                          ident[:, :])
                    tr.then_inc(tb_done[i % 2], 1)

            def h_first_unit(l, h):
                def before(n, p):
                    if (n, p) == (1, 1):
                        h_turns(l, h, (4, 5))
                    if (n, p) == (2, 1):
                        h_turns(l, h, (6, 7))
                    if p % 2 == 0:
                        pe.wait_ge(st_lo, XG_SLOTS + l * XG_LAYER + (0, XG_H2)[h]
                                   + 2 * n + p // 2 + 1)
                return before

            pe.sem_inc(w_used, RING)
            for n in range(2):
                pe.sem_inc(acc_free[n], 1)
            pe.wait_ge(ident_made, 2)
            pe.wait_ge(gains_loaded, 16)
            pe.transpose(s_bank[0][:, 0:2 * KT], rows_mix[:, :], ident[0:2 * KT, 0:2 * KT]
                         ).then_inc(gains_turned, 1)
            h_turns(0, 0, (0, 1))
            pe.wait_ge(others_loaded, 16 * 3)
            pe.transpose(s_bank[1][:, 0:4 * KT], rows_others[:, :], ident[0:4 * KT, 0:4 * KT]
                         ).then_inc(gains_turned, 1)
            h_turns(0, 0, (2, 3))

            with pe.Fori(0, DEPTH) as l:
                hu0 = l * HU_LAYER
                a0 = l * ACC_LAYER
                xg0 = XG_SLOTS + l * XG_LAYER

                unit(hu0, a0, h_hi, h_lo, h_first_unit(l, 0))
                with pe.Fori(1, 6) as u:
                    unit(hu0 + u * 2, a0 + u, h_hi, h_lo)

                def pooled(g):
                    if g >= 2:
                        pe.wait_ge(pooled_ready, l * 4 + g - 1)
                    for ct in range(2):
                        ch = g * GROUP + ct * P
                        src = [proj[:, ch // CH, t, ch % CH:ch % CH + P] for t in range(T)]
                        dst = s_bank[g % 2]
                        o = ct * SEQ
                        pe.matmul(dst[:, o:o + BAND], src[0], band[:, g, 0, :],
                                  start=True, stop=False)
                        pe.matmul(dst[:, o + BAND_AT:o + BAND], src[1],
                                  band[:, g, 1, 0:BAND - BAND_AT], start=False, stop=True)
                        mm = pe.matmul(dst[:, o + BAND:o + SEQ], src[1],
                                       band[:, g, 1, BAND - BAND_AT:BAND], start=True, stop=True)
                    mm.then_inc(pooled_done, 1)

                def pool_out(g):
                    pe.wait_ge(pooled_ready, l * 4 + g + 1)
                    if g < 2:
                        pe.wait_ge(pooled_ready, l * 4 + g + 3)
                    else:
                        pe.wait_ge(y_ready, l * 4 + g - 1)
                    for t in range(T):
                        for ct in range(2):
                            mm = pe.matmul(s_bank[g % 2][:, t * GROUP:(t + 1) * GROUP],
                                           pooled_t[:, 2 * g + ct, h_cols(t)],
                                           w_pool_s[:, 2 * g + ct, :], start=ct == 0, stop=ct == 1)
                    mm.then_inc(y_done, 1)

                def y_turn(i):
                    t, c = Y_ORDER[i]
                    pe.wait_ge(y_ready, l * 4 + 2 * c + 2)
                    if i >= 2:
                        pe.wait_ge(xg_ready, l * XG_LAYER + XG_Y + i - 1)
                    for j in range(4):
                        tr = pe.transpose(t_bank[i % 2][:, h_cols(j)],
                                          y[:, c, t, h_cols(j)], ident[:, :])
                    tr.then_inc(tb_done[i % 2], 1)

                def turn_qk(c):
                    if c == 0:
                        pe.wait_ge(rope_step, l * 12 + 12)
                    for e in range(2):
                        h = 2 * c + e
                        if c > 0:
                            pe.wait_ge(tb_free[e], l * 8 + 2 * c)
                        else:
                            pe.wait_ge(xg_ready, l * XG_LAYER + XG_Y + 3 + e)
                        for n, first_unit in enumerate((2, 4)):
                            for t in range(T):
                                tr = pe.transpose(
                                    t_bank[e][:, n * SEQ + t * P:n * SEQ + (t + 1) * P],
                                    proj[:, first_unit + h // 4, t, h_cols(h % 4)], ident[:, :])
                        tr.then_inc(tb_done[e], 1)

                def scores(c):
                    for e in range(2):
                        pe.wait_ge(tb_free[e], l * 8 + 2 * c + 1)
                        if c == 0:
                            pe.wait_ge(y_ready, l * 4 + 3 + e)
                        else:
                            pe.wait_ge(score_ready, l * HEADS + 2 * c + e - 1)
                        for t in range(T):
                            mm = pe.matmul(s_bank[e][:, t * SEQ:(t + 1) * SEQ],
                                           qk_t[:, e, h_cols(t)], qk_t[:, e, SEQ:2 * SEQ],
                                           start=True, stop=True)
                        mm.then_inc(s_done, 1)

                def turn_probs(c):
                    for e in range(2):
                        pe.wait_ge(prob_ready, l * HEADS + 2 * c + e + 1)
                        pe.wait_ge(tb_free[e], l * 8 + 2 * c + 1)
                        for kt in range(T):
                            for t in range(T):
                                tr = pe.transpose(
                                    t_bank[e][:, kt * SEQ + t * P:kt * SEQ + (t + 1) * P],
                                    probs[:, e, t, h_cols(kt)], ident[:, :])
                        tr.then_inc(tb_done[e], 1)

                def mix_values(c):
                    if c == 0:
                        for t in range(T):
                            pe.wait_ge(acc_free[t], a0 + 8 + 1)
                    else:
                        pe.wait_ge(xg_ready, l * XG_LAYER + XG_O + c)
                        pe.wait_ge(o_squared, l * 4 + c)
                    for e in range(2):
                        h = 2 * c + e
                        pe.wait_ge(tb_free[e], l * 8 + 2 * c + 2)
                        for kt in range(T):
                            mm = pe.matmul(o_bank[:, e * SEQ:(e + 1) * SEQ],
                                           proj[:, 6 + h // 4, kt, h_cols(h % 4)],
                                           probs_t[:, e, kt, :], start=kt == 0, stop=kt == 1)
                    mm.then_inc(o_done, 1)

                def with_v0(n, p):
                    if (n, p) == (0, 2):
                        for t in range(T):
                            pe.wait_ge(acc_free[t], a0 + 2 + 1)
                        pe.wait_ge(band_ready, 1)
                        pooled(0)
                        pooled(1)
                    if (n, p) == (1, 2):
                        pooled(2)
                        pooled(3)
                    if (n, p) == (2, 2):
                        pe.wait_ge(pool_w_loaded, l * 16 + 16)
                        pool_out(0)
                        pool_out(1)
                    if (n, p) == (3, 2):
                        pool_out(2)
                        pool_out(3)

                def with_v1(n, p):
                    if (n, p) == (0, 2):
                        y_turn(0)
                        y_turn(1)
                    if (n, p) == (1, 2):
                        y_turn(2)
                        y_turn(3)
                    if (n, p) == (2, 2):
                        turn_qk(0)
                    if (n, p) == (3, 0):
                        scores(0)

                unit(hu0 + 12, a0 + 6, h_hi, h_lo, with_v0)
                unit(hu0 + 14, a0 + 7, h_hi, h_lo, with_v1)

                pe.wait_ge(st_lo, xg0 + XG_O)
                for c in range(CHUNKS):
                    for t in range(T):
                        for p in range(PAIRS):
                            pair(t, p, hu0 + HU_B1 + c, c % 2, f_hi, f_lo, 8, acc_bank[t],
                                 True, True, a0 + ACC_B1 + c)
                            if (t, p) == (0, 0):
                                turn_probs(c)
                            if (t, p) == (0, 1):
                                mix_values(c)
                                if c + 1 < CHUNKS:
                                    turn_qk(c + 1)
                            if (t, p) == (0, 3) and c + 1 < CHUNKS:
                                scores(c + 1)

                for c0 in range(0, CHUNKS, 2):
                    for t in range(T):
                        for c in (c0, c0 + 1):
                            for p in range(PAIRS):
                                if c == 0 and t == 0:
                                    pe.wait_ge(st_lo, xg0 + XG_O + p + 1)
                                if (c, t, p) == (1, 0, 0):
                                    pe.wait_ge(score_ready, (l + 1) * HEADS)
                                pair(t, p, hu0 + HU_B2 + c, c % 2, f_hi, f_lo, 0,
                                     (acc_bank, s_bank)[c % 2][t], True, True,
                                     a0 + ACC_B2 + c - min(c, 1))
                                if (c, t, p) == (0, 0, 0):
                                    pe.wait_ge(o_summed, l * 4 + 4)
                                    for tt in range(T):
                                        for e in range(2):
                                            o = e * SEQ + tt * P
                                            mm = pe.matmul(ssa_bank[:, tt:tt + 1],
                                                           o_sqsum[:, o:o + P], ones[:, :],
                                                           start=e == 0, stop=e == 1)
                                    mm.then_inc(ssa_done, 1)
                                if (c, t, p) == (2, 1, 2):
                                    h_turns(l, 1, (0, 1))
                                if (c, t, p) == (3, 1, 0):
                                    h_turns(l, 1, (2, 3))

                def turn_f(g, u, t):
                    pe.wait_ge(f_ready, l * 32 + g * 8 + u * 2 + t + 1)
                    pe.wait_ge(flo_made, l * 32 + g * 8 + u * 2 + t + 1)
                    for j in range(4):
                        tr = pe.transpose(t_bank[t][:, h_cols(j)], act_f[:, t, h_cols(j)],
                                          ident[:, :])
                    tr.then_inc(tb_done[t], 1)

                def group(g, first, last):
                    hu = hu0 + HU_F + g * HU_GROUP
                    r = a0 + ACC_F + g * (2 * CHUNKS)
                    h_before = h_first_unit(l, 1) if first else None

                    def up_first(n, p):
                        if h_before is not None:
                            h_before(n, p)
                        if (n, p) == (3, 2):
                            turn_f(g, 0, 0)
                    unit(hu, r, h_hi, h_lo, up_first)
                    with pe.Fori(1, CHUNKS) as u:
                        def up_next(n, p):
                            if (n, p) == (1, 2):
                                turn_f(g, u - 1, 1)
                            if (n, p) == (3, 2):
                                turn_f(g, u, 0)
                        unit(hu + u * 2, r + u, h_hi, h_lo, up_next)

                    def down_first(n, p):
                        if (n, p) == (1, 2):
                            turn_f(g, CHUNKS - 1, 1)
                        if p == 0:
                            pe.wait_ge(flo_made, T + l * 32 + g * 8 + (3, 7, 4, 8)[n])

                    def down_last(n, p):
                        if (n, p) in ((2, 3), (3, 1)):
                            with pe.If(l < DEPTH - 1):
                                h_turns(l + 1, 0, (0, 1) if n == 2 else (2, 3))

                    unit(hu + 2 * CHUNKS, r + CHUNKS, f_hi, f_lo, down_first)
                    with pe.Fori(1, CHUNKS - 1 if last else CHUNKS) as c:
                        unit(hu + 2 * CHUNKS + c * 2, r + CHUNKS + c, f_hi, f_lo)
                    if last:
                        unit(hu + HU_GROUP - 2, r + 2 * CHUNKS - 1, f_hi, f_lo, down_last)

                group(0, True, False)
                with pe.Fori(1, FF_GROUPS - 1) as g:
                    group(g, False, False)
                group(FF_GROUPS - 1, False, True)

        @block.scalar
        def _(act):
            def split_hi(hu, half, which=range(PAIRS)):
                for p in which:
                    act.wait_ge(raw_loaded[p], hu * 16 + 16)
                    act.wait_ge(w_used, hu * PAIRS + p + 1)
                    act.copy(w_hi[:, half * PAIRS + p, :], raw[:, p, :]).then_inc(hi_made, 1)

            def stationary_hi(i, dst, slot, k):
                act.wait_ge(xg_ready, i + 1)
                act.copy(dst, xg[:, slot, :].rearrange("p (k n) -> p k n", k=k)).then_inc(st_hi, 1)

            def h_chunks(l, h, which):
                for i in which:
                    t, c = i // CHUNKS, i % CHUNKS
                    stationary_hi(l * XG_LAYER + (0, XG_H2)[h] + i,
                                  h_hi[:, 4 * c:4 * c + 4, h_cols(t)], i % 2, 4)

            def h_squares(l, h, t):
                for c in range(CHUNKS):
                    i = t * CHUNKS + c
                    act.wait_ge(x_ready, l * 16 + 8 * h + i + 1)
                    if h or i:
                        act.wait_ge(sq_done, l * SQ_LAYER + (0, SQ_H2)[h] + i)
                    act.activation(junk[:, :], x[:, t, c_cols(c)], ACT.Square,
                                   accum_out=ss_x[:, t, c:c + 1]).then_inc(sq_done, 1)

            def h_first_unit(l, h, hu):
                split_hi(hu + 1, 1, (1, 2, 3))
                h_squares(l, h, 0)
                h_chunks(l, h, range(4, 8))
                h_squares(l, h, 1)

            def take_proj(l, u, t):
                act.wait_ge(rstd_ready, T + l * RS_LAYER + RS_X1 + t + 1)
                result_stands(act, t, l * ACC_LAYER + u, l * HU_LAYER + u * 2 + 1)
                act.mul(proj_out(u, t), acc_bank[t][:, :], rstd[:, COL_X1 + t:COL_X1 + t + 1]
                        ).then_inc(acc_free[t], 1)

            def proj_out(u, t):
                if isinstance(u, int):
                    return proj[:, u, t, :]
                return proj[:, ld(u, 1), t, :].rearrange("p a c -> p (a c)")

            act.wait_ge(ones_made, 1)
            act.copy(warm[:, :], ones[:, :]).then_inc(warm_done, 1)
            x_rows = x_in[0].rearrange("(t p) d -> t p d", p=P)
            act.wait_ge(x_loaded[0], 16)
            row = 0
            for g in (g_ffn_pre, g_attn_out, g_pool_out):
                n = DEPTH * g.shape[1] // P
                act.dma_start(rows_others[row:row + n, :], g.rearrange("l (k p) -> (l k) p", p=P)
                              ).then_inc(others_loaded, 16)
                row += n
            act.dma_start(x[:, 0, D // 2:], x_rows[0][:, D // 2:]).then_inc(x_loaded[1], 16)
            act.dma_start(pos_i[:, :], positions[0].rearrange("(t p) -> p t", p=P),
                          allow_slow_non_contiguous=True).then_inc(pos_loaded, 16)
            split_hi(0, 0, (0,))
            act.dma_start(x[:, 1, :], x_rows[1]).then_inc(x_loaded[2], 16)
            h_chunks(0, 0, (0, 1))
            split_hi(0, 0, (1, 2))
            h_chunks(0, 0, (2, 3))
            split_hi(0, 0, (3,))
            split_hi(1, 1, (0,))

            with act.Fori(0, DEPTH) as l:
                hu0 = l * HU_LAYER
                a0 = l * ACC_LAYER
                xg0 = l * XG_LAYER

                h_first_unit(l, 0, hu0)
                take_proj(l, 0, 0)
                split_hi(hu0 + 2, 0)
                split_hi(hu0 + 3, 1)
                take_proj(l, 0, 1)
                with act.Fori(1, 6) as u:
                    take_proj(l, u, 0)
                    split_hi(hu0 + u * 2 + 2, 0)
                    split_hi(hu0 + u * 2 + 3, 1)
                    take_proj(l, u, 1)

                with act.If(l < 1):
                    act.wait_ge(angle_ready, 1)
                    act.activation(sin_t[:, :, :], rt[0][:, :, :], ACT.Sin
                                   ).then_inc(rope_table_ready, 1)
                    act.activation(cos_t[:, :, :], rt[1][:, :, :], ACT.Sin
                                   ).then_inc(rope_table_ready, 1)

                def take_pooled(g):
                    act.wait_ge(pooled_done, l * 4 + g + 1)
                    act.copy(pooled_t[:, 2 * g:2 * g + 2, :],
                             s_bank[g % 2][:, :].rearrange("p (c n) -> p c n", c=2)
                             ).then_inc(pooled_ready, 1)

                for g in range(4):
                    take_pooled(g)
                take_proj(l, 6, 0)
                split_hi(hu0 + 14, 0)
                split_hi(hu0 + 15, 1)
                take_proj(l, 6, 1)

                act.wait_ge(y_ready, l * 4 + 4)
                for t in range(T):
                    act.wait_ge(sq_done, l * SQ_LAYER + SQ_Y + t)
                    act.activation(junk_y[:, :, :], y[:, :, t, :], ACT.Square,
                                   accum_out=ss_p[:, t:t + 1]).then_inc(sq_done, 1)
                for i in range(4):
                    t, c = Y_ORDER[i]
                    stationary_hi(xg0 + XG_Y + i,
                                  f_hi[:, 8 + 4 * c:12 + 4 * c, h_cols(t)], i % 2, 4)

                def take_qk(c):
                    for e in range(2):
                        act.wait_ge(tb_done[e], l * TB_LAYER + TB_QK + 2 * c + 1)
                        act.copy(qk_t[:, e, :], t_bank[e][:, :]).then_inc(tb_free[e], 1)

                def exponentials(c):
                    for e in range(2):
                        h = 2 * c + e
                        act.wait_ge(max_ready, l * HEADS + h + 1)
                        for t in range(T):
                            ex = act.activation(probs[:, e, t, :], probs[:, e, t, :], ACT.Exp,
                                                bias=neg_max[:, h, t:t + 1],
                                                accum_out=den[:, h, t:t + 1])
                            ex.then_inc(exp_done, 1)

                take_proj(l, 7, 0)
                take_qk(0)
                split_hi(hu0 + 16, 0)
                exponentials(0)
                split_hi(hu0 + 17, 1, (0,))
                take_proj(l, 7, 1)

                def take_probs_t(c):
                    for e in range(2):
                        act.wait_ge(tb_done[e], l * TB_LAYER + TB_QK + 2 * c + 2)
                        act.copy(probs_t[:, e, :, :],
                                 t_bank[e][:, :].rearrange("p (k n) -> p k n", k=2)
                                 ).then_inc(tb_free[e], 1)

                def take_mix(t, c):
                    act.wait_ge(rstd_ready, T + l * RS_LAYER + RS_P + 1)
                    result_stands(act, t, a0 + ACC_B1 + c, hu0 + HU_B1 + c)
                    act.mul(acc[:, t, c_cols(c)], acc_bank[t][:, :],
                            rstd[:, COL_P + t:COL_P + t + 1]).then_inc(acc_free[t], 1)

                for c in range(CHUNKS):
                    hu = hu0 + HU_B1 + c
                    take_probs_t(c)
                    act.wait_ge(o_done, l * 4 + c + 1)
                    if c > 0:
                        act.wait_ge(o_summed, l * 4 + c)
                    act.activation(o_sq[:, :], o_bank[:, :], ACT.Square).then_inc(o_squared, 1)
                    if c + 1 < CHUNKS:
                        take_qk(c + 1)
                    if c > 0:
                        take_mix(1, c - 1)
                    stationary_hi(xg0 + XG_O + c, f_hi[:, 2 * c:2 * c + 2, :], c % 2, 2)
                    split_hi(hu + 1, 1 - c % 2, (1, 2, 3))
                    if c + 1 < CHUNKS:
                        exponentials(c + 1)
                    take_mix(0, c)
                    split_hi(hu + 2, c % 2, (0,))
                take_mix(1, CHUNKS - 1)
                split_hi(hu0 + HU_B2 + 1, 1, (1, 2, 3))

                def post_square(base, n, result, t, c):
                    act.wait_ge(acc_free[t], 1 + result + 1)
                    act.wait_ge(sq_done, l * SQ_LAYER + base + n)
                    act.activation(junk[:, :], acc[:, t, ld(c * CH, CH)], ACT.Square,
                                   accum_out=ss_post[:, t, ld(c, 1)]).then_inc(sq_done, 1)

                def mix_square(t, c):
                    post_square(SQ_B2, mix_order(t, c), a0 + ACC_B2 + c, t, c)

                mix_square(0, 0)
                mix_square(0, 1)
                split_hi(hu0 + HU_B2 + 2, 0)
                mix_square(1, 0)
                split_hi(hu0 + HU_B2 + 3, 1)
                mix_square(1, 1)

                hu_f = hu0 + HU_F
                mix_square(0, 2)
                mix_square(0, 3)
                split_hi(hu_f, 0)
                h_chunks(l, 1, (0, 1))
                mix_square(1, 2)
                h_chunks(l, 1, (2, 3))
                split_hi(hu_f + 1, 1, (0,))
                mix_square(1, 3)

                def activate(g, u, t):
                    act.wait_ge(rstd_ready, T + l * RS_LAYER + RS_X2 + t + 1)
                    result_stands(act, t, a0 + ACC_F + g * 8 + u,
                                  hu0 + HU_F + g * HU_GROUP + u * 2 + 1)
                    act.activation(act_f[:, t, :], acc_bank[t][:, :], ACT.Relu,
                                   scale=rstd[:, COL_X2 + t:COL_X2 + t + 1]
                                   ).then_inc(acc_free[t], 1)
                    act.wait_ge(acc_free[t], 1 + a0 + ACC_F + g * 8 + u + 1)
                    act.activation(act_f[:, t, :], act_f[:, t, :], ACT.Square
                                   ).then_inc(f_ready, 1)

                def f_chunk_hi(g, u, t):
                    act.wait_ge(tb_done[t], l * TB_LAYER + TB_F + g * 4 + u + 1)
                    act.copy(f_out(f_hi, u, t), t_bank[t][:, :].rearrange("p (k n) -> p k n", k=4)
                             ).then_inc(fhi_made, 1)

                def up_unit(g, u, hu):
                    activate(g, u, 0)
                    split_hi(hu + 2, 0)
                    f_chunk_hi(g, u, 0)
                    split_hi(hu + 3, 1, (0, 1, 2))
                    activate(g, u, 1)
                    split_hi(hu + 3, 1, (3,))
                    f_chunk_hi(g, u, 1)

                def group(g, first, last):
                    hu = hu0 + HU_F + g * HU_GROUP
                    if first:
                        h_first_unit(l, 1, hu)
                    with act.Fori(0, CHUNKS) as u:
                        up_unit(g, u, hu + u * 2)
                    if not last:
                        with act.Fori(0, CHUNKS) as c:
                            split_hi(hu + 8 + c * 2 + 2, 0)
                            split_hi(hu + 8 + c * 2 + 3, 1)
                        return
                    r = a0 + ACC_F + g * 8 + CHUNKS
                    with act.Fori(0, CHUNKS - 1) as c:
                        post_square(SQ_F, c * 2, r + c, 0, c)
                        split_hi(hu + 8 + c * 2 + 2, 0)
                        split_hi(hu + 8 + c * 2 + 3, 1)
                        post_square(SQ_F, c * 2 + 1, r + c, 1, c)
                    c = CHUNKS - 1
                    post_square(SQ_F, 2 * c, r + c, 0, c)
                    with act.If(l < DEPTH - 1):
                        split_hi(hu + HU_GROUP, 0)
                        h_chunks(l + 1, 0, (0, 1))
                        h_chunks(l + 1, 0, (2, 3))
                        split_hi(hu + HU_GROUP + 1, 1, (0,))
                    post_square(SQ_F, 2 * c + 1, r + c, 1, c)
                    act.wait_ge(sq_done, (l + 1) * SQ_LAYER)

                group(0, True, False)
                with act.Fori(1, FF_GROUPS - 1) as g:
                    group(g, False, False)
                group(FF_GROUPS - 1, False, True)

        @block.vector
        def _(dve):
            def split_lo(hu, half, which=range(PAIRS)):
                for p in which:
                    dve.wait_ge(hi_made, hu * PAIRS + p + 1)
                    slot = half * PAIRS + p
                    dve.tensor_tensor(w_lo[:, slot, :], raw[:, p, :],
                                      w_hi[:, slot, :].bitcast(F32), ALU.subtract
                                      ).then_inc(lo_made, 1)

            def scaled(i, slot, bank, g, k):
                dve.wait_ge(st_lo, i + 1)
                dve.tensor_tensor(
                    xg[:, slot, :].rearrange("p (k n) -> p k n", k=k),
                    bank[:, :].rearrange("p (k n) -> p k n", k=k),
                    gain[:, g:g + k, None].to_broadcast([P, k, CH // k]), ALU.mult
                    ).then_inc(xg_ready, 1)

            def mean(col, src):
                dve.tensor_scalar(src, src, 1.0 / D, EPS, ALU.mult, ALU.add,
                                  accum_out=mean_sq[:, col:col + 1]).then_inc(mean_ready, 1)

            def add_posts(l, h, which):
                for i in which:
                    t, c = i // CHUNKS, i % CHUNKS
                    col = (COL_POST2, COL_POST1)[h] + t
                    dve.wait_ge(rstd_ready, l * RS_LAYER + h * (RS_POST1 + T) + t + 1)
                    dve.wait_ge(post_ready, l * 4 * CHUNKS + h * (2 * CHUNKS)
                                + (ff_order, mix_order)[h](t, c) + 1)
                    dve.scalar_tensor_tensor(x[:, t, c_cols(c)], acc[:, t, c_cols(c)],
                                             rstd[:, col:col + 1], x[:, t, c_cols(c)],
                                             ALU.mult, ALU.add).then_inc(x_ready, 1)

            def h_chunks(l, h, which):
                for i in which:
                    dve.wait_ge(tb_done[i % 2], l * TB_LAYER + (0, TB_H2)[h] + i // 2 + 1)
                    scaled(l * XG_LAYER + (0, XG_H2)[h] + i, i % 2, t_bank[i % 2],
                           (G_MIX, G_FFN)[h] + 4 * (i % CHUNKS), 4)

            def mean_x(l, h, t):
                dve.wait_ge(sq_done, l * SQ_LAYER + (0, SQ_H2)[h] + 4 + 4 * t)
                mean((COL_X1, COL_X2)[h] + t, ss_x[:, t, :])

            def h_first_unit(l, h, hu):
                add_posts(l, h, (4, 5))
                split_lo(hu + 1, 1, (2, 3))
                mean_x(l, h, 0)
                h_chunks(l, h, (4, 5))
                add_posts(l, h, (6, 7))
                h_chunks(l, h, (6, 7))

            dve.sem_inc(lo_made, RAW)
            dve.sem_inc(flo_made, T)
            dve.memset(ones[:, :], 1.0).then_inc(ones_made, 1)
            dve.memset(rstd[:, :], 1.0).then_inc(setup_done, 1)
            dve.memset(acc[:, 1, :], 0.0).then_inc(setup_done, 1)
            dve.memset(gains_d[:, :, DEPTH, :], 0.0).then_inc(setup_done, 1)
            dve.memset(gains_half[:, :, DEPTH, :], 0.0).then_inc(setup_done, 1)
            dve.wait_ge(gains_turned, 1)
            dve.tensor_copy(gain[:, G_MIX:G_MIX + KT], s_bank[0][:, 0:KT]).then_inc(gain_ready, 1)
            dve.tensor_copy(gains_d[:, 0, 0:DEPTH, :],
                            s_bank[0][:, 0:2 * KT].rearrange("p (l k) -> p l k", l=DEPTH)
                            ).then_inc(gains_ready, 1)
            dve.wait_ge(x_loaded[0], 16)
            dve.sem_inc(x_ready, 2)
            dve.wait_ge(gain_ready, 1)
            h_chunks(0, 0, (0, 1))
            split_lo(0, 0, (0, 1))
            dve.wait_ge(x_loaded[1], 16)
            dve.sem_inc(x_ready, 2)
            h_chunks(0, 0, (2, 3))
            split_lo(0, 0, (2, 3))
            dve.wait_ge(gains_turned, 2)
            half = KT // 2
            for at_col, n, src in ((G_FFN, KT, 0), (G_ATTN, half, 2 * KT), (G_POOL, half, 3 * KT)):
                dve.tensor_copy(gain[:, at_col:at_col + n], s_bank[1][:, src:src + n]
                                ).then_inc(gain_ready, 1)
            dve.tensor_copy(gains_d[:, 1, 0:DEPTH, :],
                            s_bank[1][:, 0:2 * KT].rearrange("p (l k) -> p l k", l=DEPTH)
                            ).then_inc(gains_ready, 1)
            for n in range(2):
                src = s_bank[1][:, (2 + n) * KT:(3 + n) * KT]
                dve.tensor_copy(gains_half[:, n, 0:DEPTH, :],
                                src.rearrange("p (l k) -> p l k", l=DEPTH)).then_inc(gains_ready, 1)
            split_lo(1, 1, (0, 1))
            dve.wait_ge(gain_ready, 4)
            dve.wait_ge(gains_ready, 4)
            dve.wait_ge(setup_done, 4)
            dve.wait_ge(x_loaded[2], 16)

            with dve.Fori(0, DEPTH) as l:
                hu0 = l * HU_LAYER
                a0 = l * ACC_LAYER
                xg0 = l * XG_LAYER

                h_first_unit(l, 0, hu0)
                split_lo(hu0 + 2, 0)
                mean_x(l, 0, 1)
                split_lo(hu0 + 3, 1)
                with dve.Fori(1, 6) as u:
                    split_lo(hu0 + u * 2 + 2, 0)
                    split_lo(hu0 + u * 2 + 3, 1)

                dve.wait_ge(rope_table_ready, 2)
                dve.wait_ge(st_lo, xg0 + XG_Y + XG_SLOTS)
                hr = ROPE // 2
                for t in range(T):
                    dve.wait_ge(acc_free[t], 1 + a0 + 6)
                    qk = proj[:, 2:6, t, :].rearrange("p u (h d) -> p u h d", d=P)
                    x1, x2 = qk[:, :, :, 0:hr], qk[:, :, :, hr:ROPE]
                    cs = cos_t[:, t, None, None, :].to_broadcast([P, 4, 4, hr])
                    sn = sin_t[:, t, None, None, :].to_broadcast([P, 4, 4, hr])
                    step = l * 12 + t * 6
                    if t:
                        dve.wait_ge(rope_step, step)
                    for n, (a, b) in enumerate(((x1, cs), (x2, sn), (x2, cs), (x1, sn))):
                        dve.tensor_tensor(rope_tmp[:, n], a, b, ALU.mult).then_inc(rope_step, 1)
                    dve.wait_ge(rope_step, step + 4)
                    dve.tensor_tensor(x1, rope_tmp[:, 0], rope_tmp[:, 1], ALU.subtract
                                      ).then_inc(rope_step, 1)
                    dve.tensor_tensor(x2, rope_tmp[:, 2], rope_tmp[:, 3], ALU.add
                                      ).then_inc(rope_step, 1)
                dve.wait_ge(rope_step, l * 12 + 12)

                def scale_pooled(g):
                    dve.wait_ge(y_done, l * 4 + g + 1)
                    row = scale_row[:, g * GROUP:(g + 1) * GROUP]
                    dve.tensor_tensor(y[:, g // 2, :, (g % 2) * GROUP:(g % 2 + 1) * GROUP],
                                      s_bank[g % 2][:, :].rearrange("p (t n) -> p t n", t=T),
                                      row[:, None, :].to_broadcast([P, T, GROUP]), ALU.mult
                                      ).then_inc(y_ready, 1)

                dve.wait_ge(scale_loaded, l * 16 + 16)
                split_lo(hu0 + 14, 0, (0, 1))
                scale_pooled(0)
                scale_pooled(1)
                split_lo(hu0 + 14, 0, (2, 3))
                split_lo(hu0 + 15, 1, (0, 1))
                scale_pooled(2)
                scale_pooled(3)
                split_lo(hu0 + 15, 1, (2, 3))

                for i in range(4):
                    t, c = Y_ORDER[i]
                    dve.wait_ge(tb_done[i % 2], l * TB_LAYER + TB_Y + i // 2 + 1)
                    scaled(xg0 + XG_Y + i, i % 2, t_bank[i % 2], G_POOL + 4 * c, 4)
                for t in range(T):
                    dve.wait_ge(sq_done, l * SQ_LAYER + SQ_Y + t + 1)
                dve.tensor_scalar(mean_sq[:, COL_P:COL_P + 2], ss_p[:, :], 1.0 / HALF_W, EPS,
                                  ALU.mult, ALU.add).then_inc(mean_ready, 1)

                def masked_scores(c):
                    for e in range(2):
                        h = 2 * c + e
                        dve.wait_ge(s_done, l * HEADS + h + 1)
                        if c > 0:
                            dve.wait_ge(tb_done[e], l * TB_LAYER + TB_QK + 2 * c)
                        dve.scalar_tensor_tensor(
                            probs[:, e].rearrange("p t n -> p (t n)"), s_bank[e][:, :],
                            float(P) ** -0.5, bias[:, :, :].rearrange("p t n -> p (t n)"),
                            ALU.mult, ALU.add).then_inc(score_ready, 1)
                        dve.wait_ge(score_ready, l * HEADS + h + 1)
                        dve.tensor_reduce(neg_max[:, h, :], probs[:, e, :, :], AX.X, ALU.max,
                                          negate=True).then_inc(max_ready, 1)

                def normalised(c):
                    for e in range(2):
                        h = 2 * c + e
                        dve.wait_ge(exp_done, l * 2 * HEADS + 2 * h + 2)
                        dve.reciprocal(rden[:, h, :], den[:, h, :]).then_inc(rden_ready, 1)
                        dve.wait_ge(rden_ready, l * HEADS + h + 1)
                        dve.tensor_scalar(probs[:, e, 0, :], probs[:, e, 0, :], rden[:, h, 0:1],
                                          None, ALU.mult)
                        dve.tensor_scalar(probs[:, e, 1, :], probs[:, e, 1, :], rden[:, h, 1:2],
                                          None, ALU.mult).then_inc(prob_ready, 1)

                split_lo(hu0 + 16, 0)
                dve.wait_ge(bias_ready, 1)
                masked_scores(0)
                normalised(0)
                split_lo(hu0 + 17, 1, (0,))

                for c in range(CHUNKS):
                    hu = hu0 + HU_B1 + c
                    dve.wait_ge(o_squared, l * 4 + c + 1)
                    scaled(xg0 + XG_O + c, c % 2, o_bank, G_ATTN + 2 * c, 2)
                    if c == 0:
                        dve.tensor_copy(o_sqsum[:, :], o_sq[:, :]).then_inc(o_summed, 1)
                    else:
                        dve.wait_ge(o_summed, l * 4 + c)
                        dve.tensor_tensor(o_sqsum[:, :], o_sqsum[:, :], o_sq[:, :], ALU.add
                                          ).then_inc(o_summed, 1)
                    split_lo(hu + 1, 1 - c % 2, (1,))
                    if c + 1 < CHUNKS:
                        masked_scores(c + 1)
                        normalised(c + 1)
                    split_lo(hu + 1, 1 - c % 2, (2, 3))
                    split_lo(hu + 2, c % 2, (0,))
                split_lo(hu0 + HU_B2 + 1, 1, (1, 2, 3))

                def mixed(t, c):
                    result_stands(dve, t, a0 + ACC_B2 + c, hu0 + HU_B2 + c)
                    dve.scalar_tensor_tensor(acc[:, t, c_cols(c)],
                                             (acc_bank, s_bank)[c % 2][t][:, :],
                                             rstd[:, COL_A + t:COL_A + t + 1],
                                             acc[:, t, c_cols(c)], ALU.mult, ALU.add
                                             ).then_inc(acc_free[t], 1)

                def mean_post(base, n, col, t):
                    dve.wait_ge(sq_done, l * SQ_LAYER + base + n + 1)
                    mean(col + t, ss_post[:, t, :])

                dve.wait_ge(ssa_done, l + 1)
                dve.tensor_scalar(mean_sq[:, COL_A:COL_A + 2], ssa_bank[:, 0:2],
                                  1.0 / HALF_W, EPS, ALU.mult, ALU.add).then_inc(mean_ready, 1)
                dve.wait_ge(rstd_ready, T + l * RS_LAYER + RS_A + 1)
                mixed(0, 0)
                mixed(0, 1)
                split_lo(hu0 + HU_B2 + 2, 0)
                mixed(1, 0)
                split_lo(hu0 + HU_B2 + 3, 1)
                mixed(1, 1)

                hu_f = hu0 + HU_F
                mixed(0, 2)
                mixed(0, 3)
                mean_post(SQ_B2, mix_order(0, 3), COL_POST1, 0)
                add_posts(l, 1, range(4))
                h_chunks(l, 1, (0, 1))
                split_lo(hu_f, 0, (0, 1, 2))
                mixed(1, 2)
                h_chunks(l, 1, (2, 3))
                split_lo(hu_f, 0, (3,))
                mixed(1, 3)
                split_lo(hu_f + 1, 1, (0,))
                mean_post(SQ_B2, mix_order(1, 3), COL_POST1, 1)
                split_lo(hu_f + 1, 1, (1,))

                def f_chunk_lo(g, u, t):
                    dve.wait_ge(fhi_made, l * 32 + g * 8 + u * 2 + t + 1)
                    dve.tensor_tensor(f_out(f_lo, u, t),
                                      t_bank[t][:, :].rearrange("p (k n) -> p k n", k=4),
                                      f_out(f_hi, u, t).bitcast(F32), ALU.subtract
                                      ).then_inc(flo_made, 1)

                def down_sum(g, c, t, first):
                    result_stands(dve, t, a0 + ACC_F + g * 8 + CHUNKS + c,
                                  hu0 + HU_F + g * HU_GROUP + 2 * CHUNKS + c * 2 + 1)
                    dst = acc[:, t, ld(c * CH, CH)]
                    if first:
                        dve.tensor_copy(dst, acc_bank[t][:, :]).then_inc(acc_free[t], 1)
                    else:
                        dve.tensor_tensor(dst, acc_bank[t][:, :], dst, ALU.add
                                          ).then_inc(acc_free[t], 1)

                def group(g, first, last):
                    hu = hu0 + HU_F + g * HU_GROUP

                    def up_unit(u, at_start):
                        split_lo(hu + u * 2 + 2, 0)
                        if at_start:
                            mean_x(l, 1, 1)
                        f_chunk_lo(g, u, 0)
                        split_lo(hu + u * 2 + 3, 1)
                        f_chunk_lo(g, u, 1)

                    if first:
                        h_first_unit(l, 1, hu)
                        up_unit(0, True)
                    with dve.Fori(1 if first else 0, CHUNKS) as u:
                        up_unit(u, False)
                    with dve.Fori(0, CHUNKS - 1 if last else CHUNKS) as c:
                        down_sum(g, c, 0, first)
                        split_lo(hu + 8 + c * 2 + 2, 0)
                        split_lo(hu + 8 + c * 2 + 3, 1)
                        down_sum(g, c, 1, first)
                    if not last:
                        return
                    c = CHUNKS - 1
                    for src, at_col in ((gains_d, G_MIX), (gains_half, G_ATTN)):
                        n = 2 * src.shape[3]
                        dve.tensor_copy(gain[:, at_col:at_col + n],
                                        src[:, :, ld(l + 1, 1), :].rearrange("p y a k -> p (y a) k")
                                        ).then_inc(gain_ready, 1)
                    down_sum(g, c, 0, first)
                    mean_post(SQ_F, ff_order(0, c), COL_POST2, 0)
                    add_posts(l + 1, 0, range(4))
                    with dve.If(l < DEPTH - 1):
                        dve.wait_ge(gain_ready, 4 + 2 * l + 2)
                        h_chunks(l + 1, 0, (0, 1))
                        split_lo(hu + HU_GROUP, 0, (0, 1, 2))
                        h_chunks(l + 1, 0, (2, 3))
                        split_lo(hu + HU_GROUP, 0, (3,))
                    down_sum(g, c, 1, first)
                    with dve.If(l < DEPTH - 1):
                        split_lo(hu + HU_GROUP + 1, 1, (0,))
                    mean_post(SQ_F, ff_order(1, c), COL_POST2, 1)
                    with dve.If(l < DEPTH - 1):
                        split_lo(hu + HU_GROUP + 1, 1, (1,))

                group(0, True, False)
                with dve.Fori(1, FF_GROUPS - 1) as g:
                    group(g, False, False)
                group(FF_GROUPS - 1, False, True)

            add_posts(DEPTH, 0, range(4, 8))

        @block.gpsimd
        def _(pool):
            def stationary_lo(i, hi, lo, slot, k):
                pool.wait_ge(st_hi, i + 1)
                pool.tensor_tensor(lo, xg[:, slot, :].rearrange("p (k n) -> p k n", k=k),
                                   hi.bitcast(F32), ALU.subtract).then_inc(st_lo, 1)

            def h_chunks(l, h, which):
                for i in which:
                    t, c = i // CHUNKS, i % CHUNKS
                    stationary_lo(l * XG_LAYER + (0, XG_H2)[h] + i,
                                  h_hi[:, 4 * c:4 * c + 4, h_cols(t)],
                                  h_lo[:, 4 * c:4 * c + 4, h_cols(t)], i % 2, 4)

            def h_first_unit(l, h):
                root(l, (RS_X1, RS_X2)[h], (COL_X1, COL_X2)[h])
                h_chunks(l, h, range(4, 8))
                root(l, (RS_X1, RS_X2)[h] + 1, (COL_X1, COL_X2)[h] + 1)

            def root(l, rs, col, n=1):
                pool.wait_ge(mean_ready, l * RS_LAYER + rs + 1)
                pool.tensor_tensor(rstd[:, col:col + n], mean_sq[:, col:col + n],
                                   minus_half[:, 0:n], ALU.pow).then_inc(rstd_ready, 1)

            def post_gain(l, h, t, c):
                pool.wait_ge(sq_done, l * SQ_LAYER + (SQ_F, SQ_B2)[h]
                             + (ff_order, mix_order)[h](t, c) + 1)
                part = acc[:, t, c_cols(c)]
                pool.tensor_tensor(part, part, post_row[:, c_cols(c)], ALU.mult
                                   ).then_inc(post_ready, 1)

            pool.sem_inc(st_lo, XG_SLOTS)
            pool.sem_inc(rstd_ready, T)
            pool.sem_inc(post_ready, T_INIT)
            pool.memset(ident[:, :], 0.0).then_inc(ident_made, 1)
            pool.memset(minus_half[:, :], -0.5).then_inc(table_step, 1)
            pool.wait_ge(ident_made, 1)
            pool.affine_select(ident[:, :], ident[:, :], [[-1, P]], ALU.not_equal, 1.0, base=0,
                               channel_multiplier=1).then_inc(ident_made, 1)
            pool.wait_ge(table_step, 1)

            steps = [1]

            def step(ins):
                steps[0] += 1
                ins.then_inc(table_step, 1)
                pool.wait_ge(table_step, steps[0])

            def rope_tables():
                ang, theta_c, r, turns, p1, p2 = (a[:, :, :] for a in rt)
                q = rt_i[:, :, :]
                half = ROPE // 2
                inv = THETA ** (-np.arange(0, ROPE, 2, dtype=np.float64) / ROPE)
                inv = inv.astype(np.float32)
                for n in range(half):
                    step(pool.memset(freq[:, n:n + 1], float(inv[n])))
                pool.wait_ge(pos_loaded, 16)
                step(pool.tensor_copy(pos_f[:, :], pos_i[:, :]))
                for t in range(T):
                    step(pool.tensor_scalar(rt[2][:, t, :], freq[:, :], pos_f[:, t:t + 1], None,
                                            ALU.mult))
                step(pool.memset(turns, 0.0))
                for unit in (2.0 ** 20, 2.0 ** 9):
                    step(pool.tensor_scalar(q, r, 1.0 / unit, None, ALU.mult))
                    step(pool.tensor_copy(p1, q))
                    step(pool.tensor_scalar(p2, p1, unit, None, ALU.mult))
                    step(pool.tensor_tensor(r, r, p2, ALU.subtract))
                    whole = unit / (2 * np.pi)
                    part = whole - round(whole)
                    c1 = trunc_bits(part, 12)
                    c2 = trunc_bits(part - c1, 12)
                    c3 = part - c1 - c2
                    step(pool.tensor_scalar(p2, p1, c1, None, ALU.mult))
                    step(pool.tensor_copy(q, p2))
                    step(pool.tensor_copy(ang, q))
                    step(pool.tensor_tensor(p2, p2, ang, ALU.subtract))
                    step(pool.tensor_tensor(turns, turns, p2, ALU.add))
                    for part in (c2, c3):
                        step(pool.tensor_scalar(p2, p1, float(part), None, ALU.mult))
                        step(pool.tensor_tensor(turns, turns, p2, ALU.add))
                step(pool.tensor_scalar(p1, r, float(1 / (2 * np.pi)), None, ALU.mult))
                step(pool.tensor_tensor(p1, p1, turns, ALU.add))
                step(pool.tensor_copy(q, p1))
                step(pool.tensor_copy(p1, q))
                c1 = trunc_bits(2 * np.pi, 16)
                c2 = trunc_bits(2 * np.pi - c1, 16)
                for part in (c1, c2, 2 * np.pi - c1 - c2):
                    step(pool.tensor_scalar(p2, p1, float(part), None, ALU.mult))
                    step(pool.tensor_tensor(r, r, p2, ALU.subtract))
                step(pool.tensor_scalar(p2, turns, float(2 * np.pi), None, ALU.mult))
                step(pool.tensor_tensor(r, r, p2, ALU.add))
                step(pool.tensor_scalar(ang, r, 3.1415925, -3.1415925, ALU.min, ALU.max))
                step(pool.tensor_scalar(p1, ang, 0.0, None, ALU.max))
                step(pool.tensor_scalar(p2, ang, 0.0, None, ALU.min))
                step(pool.tensor_tensor(p1, p1, p2, ALU.subtract))
                pool.tensor_scalar(theta_c, p1, -1.0, float(np.pi / 2), ALU.mult, ALU.add
                                   ).then_inc(angle_ready, 1)

            def bias_table():
                b = bias[:, :, :]
                d, m, c = (a[:, :, :] for a in tmp)
                step(pool.iota(tmp_i[:, :, :], [[-P, T], [1, SEQ]], base=SEQ,
                               channel_multiplier=-1))
                step(pool.tensor_copy(d, tmp_i[:, :, :]))
                step(pool.tensor_scalar(m, d, float(SEQ - 64), None, ALU.is_ge))
                step(pool.tensor_scalar(c, d, float(SEQ + 64), None, ALU.is_le))
                step(pool.tensor_tensor(c, c, m, ALU.mult))
                for dilation in (4, 16):
                    step(pool.tensor_scalar(tmp_i[:, :, :], d, 1.0 / dilation,
                                            -(dilation - 1) / (2.0 * dilation), ALU.mult, ALU.add))
                    step(pool.tensor_copy(m, tmp_i[:, :, :]))
                    step(pool.tensor_scalar(m, m, float(dilation), None, ALU.mult))
                    step(pool.tensor_tensor(m, d, m, ALU.subtract))
                    step(pool.tensor_scalar(m, m, 0.0, None, ALU.is_equal))
                    step(pool.tensor_tensor(c, c, m, ALU.add))
                step(pool.tensor_scalar(b, c, 0.0, NEG_BIG, ALU.is_equal, ALU.mult))
                for n in (2, 3):
                    step(pool.tensor_scalar(m, c, float(n), float(np.log(n)), ALU.is_equal,
                                            ALU.mult))
                    step(pool.tensor_tensor(b, b, m, ALU.add))
                pool.sem_inc(bias_ready, 1)

            def band_table():
                eye = tmp[0][:, :, 0:BAND]
                row = tmp[1][:, 0, :]
                step(pool.memset(eye, 0.0))
                step(pool.affine_select(eye, eye, [[BAND_AT - P, T], [1, BAND]], ALU.not_equal, 1.0,
                                        base=0, channel_multiplier=-1))
                for n, w in enumerate(WINDOWS):
                    h = w // 2
                    step(pool.memset(row, 1.0 / w))
                    for i in range(h):
                        step(pool.memset(row[:, i:i + 1], 1.0 / (i + h)))
                    for i in range(SEQ - h + 1, SEQ):
                        step(pool.memset(row[:, i:i + 1], 1.0 / (SEQ - i + h)))
                    for jt in range(T):
                        b = band[:, n, jt, :]
                        at_i = jt * (BAND_AT - P)
                        step(pool.affine_select(b, row[:, jt * BAND_AT:jt * BAND_AT + BAND],
                                                [[-1, BAND]], ALU.is_ge, 0.0, base=h - at_i,
                                                channel_multiplier=1))
                        step(pool.affine_select(b, b, [[1, BAND]], ALU.is_ge, 0.0,
                                                base=at_i + h - 1, channel_multiplier=-1))
                        step(pool.tensor_tensor(b, b, eye[:, jt, :], ALU.subtract))
                pool.sem_inc(band_ready, 1)

            h_chunks(0, 0, range(4))

            with pool.Fori(0, DEPTH) as l:
                xg0 = l * XG_LAYER
                h_first_unit(l, 0)
                with pool.If(l < 1):
                    rope_tables()
                    bias_table()
                    band_table()
                for i in range(4):
                    t, c = Y_ORDER[i]
                    stationary_lo(xg0 + XG_Y + i, f_hi[:, 8 + 4 * c:12 + 4 * c, h_cols(t)],
                                  f_lo[:, 8 + 4 * c:12 + 4 * c, h_cols(t)], i % 2, 4)
                root(l, RS_P, COL_P, 2)
                for c in range(CHUNKS):
                    stationary_lo(xg0 + XG_O + c, f_hi[:, 2 * c:2 * c + 2, :],
                                  f_lo[:, 2 * c:2 * c + 2, :], c % 2, 2)
                root(l, RS_A, COL_A, 2)

                pool.wait_ge(post_row_loaded, l * 32 + 16)
                for t, c in ((0, 0), (0, 1), (1, 0), (1, 1), (0, 2)):
                    post_gain(l, 1, t, c)
                root(l, RS_POST1, COL_POST1)
                post_gain(l, 1, 0, 3)
                h_chunks(l, 1, range(4))
                post_gain(l, 1, 1, 2)
                root(l, RS_POST1 + 1, COL_POST1 + 1)
                post_gain(l, 1, 1, 3)
                h_first_unit(l, 1)

                pool.wait_ge(post_row_loaded, l * 32 + 32)
                for c in range(CHUNKS - 1):
                    for t in range(T):
                        post_gain(l, 0, t, c)
                root(l, RS_POST2, COL_POST2)
                post_gain(l, 0, 0, CHUNKS - 1)
                with pool.If(l < DEPTH - 1):
                    h_chunks(l + 1, 0, range(4))
                root(l, RS_POST2 + 1, COL_POST2 + 1)
                post_gain(l, 0, 1, CHUNKS - 1)


_INS = ("x", "positions", "g_mix_pre", "w_in", "g_attn_out", "w_pool", "pool_scale", "g_pool_out",
        "w_out", "g_mix_post", "g_ffn_pre", "w_up", "w_down", "g_ffn_post")


def kernel(**inputs):
    import concourse.bacc as bacc
    from concourse.bass_utils import run_bass_kernel_spmd

    nc = bacc.Bacc("TRN2", target_bir_lowering=False, num_devices=1, dynamic_dma_scratch_size=1024)
    arrays, args = {}, []
    for name in _INS:
        a = np.ascontiguousarray(inputs[name])
        arrays[f"in_{name}"] = a
        args.append(nc.dram_tensor(f"in_{name}", a.shape, mybir.dt.from_np(a.dtype),
                                   kind="ExternalInput").ap())
    out = nc.dram_tensor("out", (1, SEQ, D), F32, kind="ExternalOutput").ap()
    build(nc, *args, out)
    r = run_bass_kernel_spmd(nc, [arrays], core_ids=[0])
    return r.results[0]["out"]
```
